# Optimizing a Trainium2 kernel written in Bass

```python
import jax, jax.numpy as jnp
from jax import lax
import numpy as np

D_MODEL = 1024
BATCH = 1
SEQ = 256
DEPTH = 1

HEAD_DIM = 64
N_HEADS_A = 8
N_KV_HEADS_A = 2
N_HEADS_B = 8
MIX_WIDTH = (N_HEADS_A + N_HEADS_B) * HEAD_DIM
DILATED_BRANCHES = ((128, 1), (512, 4), (2048, 16))
Q_BLOCK = 128
GRID_W = 64
ROPE_THETA = 10000.0
N_EXPERTS = 32
TOP_K = 4
D_FF = D_MODEL
SWIGLU_LIMIT = 7.0
SWIGLU_ALPHA = 1.702
EXPERT_BLOCK = 128
EPS = 1e-6

SPLIT_SIZES = (N_HEADS_A * HEAD_DIM, N_KV_HEADS_A * HEAD_DIM, N_KV_HEADS_A * HEAD_DIM,
               N_HEADS_B * HEAD_DIM, N_HEADS_B * HEAD_DIM, N_HEADS_B * HEAD_DIM)
IN_WIDTH = sum(SPLIT_SIZES)
SPLIT_POINTS = tuple(int(v) for v in np.cumsum(SPLIT_SIZES)[:-1])

kernel_name = "hymba_grid_dilated_moe_encoder"

def rms_norm(x, g):
    x32 = x.astype(jnp.float32)
    y = x32 * lax.rsqrt(jnp.mean(x32 * x32, axis=-1, keepdims=True) + EPS)
    return (y * g.astype(jnp.float32)).astype(x.dtype)

def rope_angles(pos, dim):
    inv = ROPE_THETA ** (-jnp.arange(0, dim, 2, dtype=jnp.float32) / dim)
    return pos.astype(jnp.float32)[:, None] * inv[None, :]

def apply_rope(x, ang):
    c = jnp.cos(ang)[None, :, None, :].astype(x.dtype)
    s = jnp.sin(ang)[None, :, None, :].astype(x.dtype)
    x1, x2 = jnp.split(x, 2, axis=-1)
    return jnp.concatenate([x1 * c - x2 * s, x2 * c + x1 * s], axis=-1)

def axial_rope(x, ang_row, ang_col):
    half = HEAD_DIM // 2
    return jnp.concatenate([apply_rope(x[..., :half], ang_row),
                            apply_rope(x[..., half:], ang_col)], axis=-1)

def grid_attention(q, k, v):
    B, S = q.shape[:2]
    G = N_HEADS_A // N_KV_HEADS_A
    nq = S // Q_BLOCK
    scale = HEAD_DIM ** -0.5
    qb = q.reshape(B, nq, Q_BLOCK, N_KV_HEADS_A, G, HEAD_DIM).transpose(1, 0, 2, 3, 4, 5)

    def block(qi):
        s = jnp.einsum('bqhgd,bkhd->bhgqk', qi, k).astype(jnp.float32) * scale
        p = jax.nn.softmax(s, axis=-1).astype(v.dtype)
        return jnp.einsum('bhgqk,bkhd->bqhgd', p, v)

    o = lax.map(block, qb)
    return o.transpose(1, 0, 2, 3, 4, 5).reshape(B, S, N_HEADS_A * HEAD_DIM)

def dilated_attention(q, k, v):
    B, S, H, _ = q.shape
    nq = S // Q_BLOCK
    scale = HEAD_DIM ** -0.5

    def block(i):
        start = i * Q_BLOCK
        qi = lax.dynamic_slice_in_dim(q, start, Q_BLOCK, axis=1)
        t = start + jnp.arange(Q_BLOCK)
        outs, lses = [], []
        for window, dil in DILATED_BRANCHES:
            r = window // (2 * dil)
            idx = t[:, None] + dil * jnp.arange(-r, r + 1)[None, :]
            valid = (idx >= 0) & (idx < S)
            idxc = jnp.clip(idx, 0, S - 1)
            kg = jnp.take(k, idxc, axis=1)
            vg = jnp.take(v, idxc, axis=1)
            s = jnp.einsum('bqhd,bqjhd->bhqj', qi, kg).astype(jnp.float32) * scale
            s = jnp.where(valid[None, None], s, -1e30)
            lse = jax.nn.logsumexp(s, axis=-1, keepdims=True)
            p = jnp.exp(s - lse).astype(v.dtype)
            outs.append(jnp.einsum('bhqj,bqjhd->bqhd', p, vg))
            lses.append(lse[..., 0])
        w = jax.nn.softmax(jnp.stack(lses, axis=0), axis=0)
        w = w.transpose(0, 1, 3, 2)[..., None].astype(v.dtype)
        return jnp.sum(jnp.stack(outs, axis=0) * w, axis=0)

    o = lax.map(block, jnp.arange(nq))
    return o.transpose(1, 0, 2, 3, 4).reshape(B, S, H * HEAD_DIM)

def moe_ffn(h, w_router, b_router, w_gate, b_gate, w_up, b_up, w_down, b_down):
    N, D = h.shape
    logits = (h @ w_router + b_router).astype(jnp.float32)
    top_vals, top_idx = lax.top_k(logits, TOP_K)
    gates = jax.nn.softmax(top_vals, axis=-1)

    NK = N * TOP_K
    e_flat = top_idx.reshape(NK)
    tok_flat = jnp.arange(NK) // TOP_K
    g_flat = gates.reshape(NK)
    order = jnp.argsort(e_flat)
    e_sorted, tok_sorted, g_sorted = e_flat[order], tok_flat[order], g_flat[order]

    counts = jax.ops.segment_sum(jnp.ones((NK,), jnp.int32), e_flat, num_segments=N_EXPERTS)
    starts = jnp.cumsum(counts) - counts
    pad_counts = (counts + EXPERT_BLOCK - 1) // EXPERT_BLOCK * EXPERT_BLOCK
    pad_ends = jnp.cumsum(pad_counts)
    pad_starts = pad_ends - pad_counts
    dest = pad_starts[e_sorted] + (jnp.arange(NK) - starts[e_sorted])

    NB = (NK + EXPERT_BLOCK - 1) // EXPERT_BLOCK + N_EXPERTS
    rows = NB * EXPERT_BLOCK
    row_tok = jnp.zeros((rows,), jnp.int32).at[dest].set(tok_sorted)
    row_w = jnp.zeros((rows,), jnp.float32).at[dest].set(g_sorted)
    block_e = jnp.clip(jnp.searchsorted(pad_ends, jnp.arange(NB) * EXPERT_BLOCK, side='right'),
                       0, N_EXPERTS - 1)

    def expert_block(args):
        e, toks, wts = args
        xb = h[toks]
        g = xb @ w_gate[e] + b_gate[e]
        u = xb @ w_up[e] + b_up[e]
        g = jnp.minimum(g, SWIGLU_LIMIT)
        u = jnp.clip(u, -SWIGLU_LIMIT, SWIGLU_LIMIT)
        act = (u + 1.0) * (g * jax.nn.sigmoid(SWIGLU_ALPHA * g))
        return (act @ w_down[e] + b_down[e]) * wts[:, None].astype(h.dtype)

    ys = lax.map(expert_block, (block_e, row_tok.reshape(NB, EXPERT_BLOCK),
                                row_w.reshape(NB, EXPERT_BLOCK)))
    return jax.ops.segment_sum(ys.reshape(rows, D), row_tok, num_segments=N)

def setup_inputs(seed: int = 0) -> dict:
    key = jax.random.key(seed)
    ks = jax.random.split(key, 20)
    f32 = jnp.float32
    nrm = lambda k, shape, s: jax.random.normal(k, shape, f32) * s
    gain = lambda k, shape: 1.0 + 0.1 * jax.random.normal(k, shape, f32)
    L, E = DEPTH, N_EXPERTS
    return {
        "x": jax.random.normal(ks[0], (BATCH, SEQ, D_MODEL), f32),
        "attn_norm": gain(ks[1], (L, D_MODEL)),
        "w_in": nrm(ks[2], (L, D_MODEL, IN_WIDTH), D_MODEL ** -0.5),
        "q_norm": gain(ks[3], (L, HEAD_DIM)),
        "k_norm": gain(ks[4], (L, HEAD_DIM)),
        "out_norm_a": gain(ks[5], (L, N_HEADS_A * HEAD_DIM)),
        "out_norm_b": gain(ks[6], (L, N_HEADS_B * HEAD_DIM)),
        "w_out": nrm(ks[7], (L, MIX_WIDTH, D_MODEL), MIX_WIDTH ** -0.5),
        "ffn_norm": gain(ks[8], (L, D_MODEL)),
        "w_router": nrm(ks[9], (L, D_MODEL, E), D_MODEL ** -0.5),
        "b_router": nrm(ks[10], (L, E), 0.01),
        "w_gate": nrm(ks[11], (L, E, D_MODEL, D_FF), D_MODEL ** -0.5),
        "b_gate": nrm(ks[12], (L, E, D_FF), 0.01),
        "w_up": nrm(ks[13], (L, E, D_MODEL, D_FF), D_MODEL ** -0.5),
        "b_up": nrm(ks[14], (L, E, D_FF), 0.01),
        "w_down": nrm(ks[15], (L, E, D_FF, D_MODEL), D_FF ** -0.5),
        "b_down": nrm(ks[16], (L, E, D_MODEL), 0.01),
        "final_norm": gain(ks[17], (D_MODEL,)),
    }

def reference(x, attn_norm, w_in, q_norm, k_norm, out_norm_a, out_norm_b, w_out,
              ffn_norm, w_router, b_router, w_gate, b_gate, w_up, b_up, w_down, b_down,
              final_norm):
    B, S, D = x.shape
    ROWS = S // GRID_W
    pos = jnp.arange(S)
    row = jnp.repeat(jnp.arange(ROWS), GRID_W)
    col = jnp.tile(jnp.arange(GRID_W), ROWS)
    ang_row = rope_angles(row, HEAD_DIM // 2)
    ang_col = rope_angles(col, HEAD_DIM // 2)
    ang_1d = rope_angles(pos, HEAD_DIM)

    for l in range(DEPTH):
        hn = rms_norm(x, attn_norm[l])
        proj = hn @ w_in[l]
        qa, ka, va, qb, kb, vb = jnp.split(proj, SPLIT_POINTS, axis=-1)
        qa = qa.reshape(B, S, N_HEADS_A, HEAD_DIM)
        ka = ka.reshape(B, S, N_KV_HEADS_A, HEAD_DIM)
        va = va.reshape(B, S, N_KV_HEADS_A, HEAD_DIM)
        qa = axial_rope(rms_norm(qa, q_norm[l]), ang_row, ang_col)
        ka = axial_rope(rms_norm(ka, k_norm[l]), ang_row, ang_col)
        oa = grid_attention(qa, ka, va)

        qb = apply_rope(qb.reshape(B, S, N_HEADS_B, HEAD_DIM), ang_1d)
        kb = apply_rope(kb.reshape(B, S, N_HEADS_B, HEAD_DIM), ang_1d)
        vb = vb.reshape(B, S, N_HEADS_B, HEAD_DIM)
        ob = dilated_attention(qb, kb, vb)

        mix = jnp.concatenate([rms_norm(oa, out_norm_a[l]), rms_norm(ob, out_norm_b[l])], axis=-1)
        x = x + mix @ w_out[l]

        hf = rms_norm(x, ffn_norm[l]).reshape(B * S, D)
        y = moe_ffn(hf, w_router[l], b_router[l], w_gate[l], b_gate[l],
                    w_up[l], b_up[l], w_down[l], b_down[l])
        x = x + y.reshape(B, S, D).astype(x.dtype)

    return rms_norm(x, final_norm)


_drawn_inputs = setup_inputs


def setup_inputs(seed=0):
    import zlib

    import numpy as np

    out = dict(_drawn_inputs(seed))
    spreads = {}
    factors = {'b_gate': 8.0, 'b_up': 24.16, 'b_down': 8.0}
    for name, (base, spread) in spreads.items():
        noise = np.random.default_rng([zlib.crc32(name.encode()), seed]).standard_normal(out[name].shape)
        drawn = base * np.exp(spread * noise) if base else spread * noise
        out[name] = __import__('jax').numpy.asarray(drawn.astype(out[name].dtype))
    for name, factor in factors.items():
        out[name] = (out[name] * factor).astype(out[name].dtype)
    return out
```

```python
from contextlib import ExitStack

import concourse.bass as bass
import numpy as np
from concourse import mybir

ALU = mybir.AluOpType
ACT = mybir.ActivationFunctionType
AX = mybir.AxisListType
F32 = mybir.dt.float32
I32 = mybir.dt.int32

P = 128
SEQ = 256
D = 1024
TC = SEQ // P
KC = D // P
HD = 64
HEADS_A, KV_A, HEADS_B = 8, 2, 8
HEADS = HEADS_A + HEADS_B
GROUP_A = HEADS_A // KV_A
BRANCHES = ((128, 1), (512, 4), (2048, 16))
GRID_W = 64
THETA = 10000.0
E = 32
TOP_K = 4
F = 1024
FC = F // P
LIMIT = 7.0
ALPHA = 1.702
EPS = 1e-6
SCALE = HD ** -0.5

SLOTS = 64
MAX_PASSES = E + SEQ * TOP_K // SLOTS - 1
TABLE = MAX_PASSES + 1
UNITS = 12
UNIT = 2 * F
NOT_ROUTED = -16384.0

C_ID = 0
C_TRI = C_ID + P
C_TRI_IN = C_TRI + P
C_ONE = C_TRI_IN + E
C_IOTA = C_ONE + P
C_COSA = C_IOTA + 2 * SLOTS
C_SINA = C_COSA + TC * HD
C_COSB = C_SINA + TC * HD
C_SINB = C_COSB + TC * HD
C_LOGM = C_SINB + TC * HD
C_END = C_LOGM + TC * SEQ

PROJ = (
    ("qa", 0, 512, 0),
    ("kva", 512, 256, 2),
    ("vb", 1792, 512, 3),
    ("qb", 768, 512, 5),
    ("kb", 1280, 512, 7),
)
PROJ_UNITS = 9
PROJ_BANK = (4, 5, 6, 7, 0, 1, 5, 6, 7, 0)
S_BANK = (3, 4, 1)
PT_BANK = (5, 6)
O_BANK = (7, 0)
OP_BANK = (5, 6, 7, 0)
SP_BANK = (7, 6, 3, 4)

R_MAX = 3
R_SEL = 14
R_NPASS = 20
R_WT = 22
R_PICK = 28
R_PSUM = 31


def constants():
    c = np.zeros((P, C_END), np.float32)
    c[:, C_ID:C_ID + P] = np.eye(P)
    t = np.arange(P)
    c[:, C_TRI:C_TRI + P] = t[:, None] < t[None, :]
    e = np.arange(E)
    c[:E, C_TRI_IN:C_TRI_IN + E] = e[:, None] <= e[None, :]
    c[:, C_ONE:C_ONE + P] = 1.0
    c[:, C_IOTA:C_IOTA + 2 * SLOTS] = np.arange(2 * SLOTS) % SLOTS
    pos = np.arange(SEQ)

    def angles(at, dim):
        inv = np.float32(THETA) ** (-np.arange(0, dim, 2, dtype=np.float32) / np.float32(dim))
        return at.astype(np.float32)[:, None] * inv[None, :].astype(np.float32)

    row, col, one = angles(pos // GRID_W, HD // 2), angles(pos % GRID_W, HD // 2), angles(pos, HD)
    cos_a = np.concatenate([np.cos(row), np.cos(row), np.cos(col), np.cos(col)], 1)
    sin_a = np.concatenate([-np.sin(row), np.sin(row), -np.sin(col), np.sin(col)], 1)
    cos_b = np.concatenate([np.cos(one), np.cos(one)], 1)
    sin_b = np.concatenate([-np.sin(one), np.sin(one)], 1)
    for at, table in ((C_COSA, cos_a), (C_SINA, sin_a), (C_COSB, cos_b), (C_SINB, sin_b)):
        c[:, at:at + TC * HD] = table.reshape(TC, P, HD).transpose(1, 0, 2).reshape(P, TC * HD)
    delta = pos[None, :] - pos[:, None]
    times = sum(((delta % dil == 0) & (abs(delta) <= window // 2)).astype(np.float32)
                for window, dil in BRANCHES)
    logm = np.where(times > 0, np.log(np.maximum(times, 1.0)), -1e30).astype(np.float32)
    c[:, C_LOGM:C_END] = logm.reshape(TC, P, SEQ).transpose(1, 0, 2).reshape(P, TC * SEQ)
    return c


def encoder_kernel(nc, x, attn_norm, w_in, q_norm, k_norm, out_norm_a, out_norm_b, w_out,
                   ffn_norm, w_router, b_router, w_gate, b_gate, w_up, b_up, w_down, b_down,
                   final_norm, consts, out):
    with ExitStack() as ctx:
        def sb(name, shape, dt=F32):
            return ctx.enter_context(nc.sbuf_tensor(name, shape, dt))

        def sem(name):
            return ctx.enter_context(nc.semaphore(name))

        ring = sb("ring", [P, UNITS * UNIT])
        wout = sb("wout", [P, KC, D])
        acc = sb("acc", [P, TC, D])
        xs = sb("xs", [P, TC, D])
        hT = sb("hT", [P, KC, SEQ])
        qr = sb("qr", [P, TC, HEADS * HD])
        kr = sb("kr", [P, TC, (KV_A + HEADS_B) * HD])
        vv = sb("vv", [P, TC, (KV_A + HEADS_B) * HD])
        qT = sb("qT", [P, HEADS // 2, SEQ])
        kT = sb("kT", [P, (KV_A + HEADS_B) // 2, SEQ])
        work = sb("work", [P, 4, 512])
        masked = hT[:, 0:4, :].rearrange("p (b c) k -> p b c k", b=2)
        cst = sb("cst", [P, C_END])
        vecs = sb("vecs", [3 * KC, P])
        gains = sb("gains", [P, 3 * KC])
        fgain = kT[:, 0:4, :].rearrange("p k s -> p (k s)")
        qkg = sb("qkg", [P, 2, HD])
        rot = sb("rot", [P, 2, 2, TC, HD])
        wr = sb("wr", [P, KC, E])
        brt = sb("brt", [P, E])
        bg = qr[0:E, 0, :]
        bu = qr[0:E, 1, :]
        bd = kr[0:E, :, 0:512]
        ss = sb("ss", [P, 16])
        ms = sb("ms", [P, 16])
        rt = sb("rt", [P, 16])
        rstd = sb("rstd", [P, 16])
        hss = sb("hss", [P, 4, HEADS_A])
        hms = sb("hms", [P, 4, HEADS_A])
        hrt = sb("hrt", [P, 4, HEADS_A])
        hrs = sb("hrs", [P, 4, HEADS_A])
        mx = sb("mx", [P, HEADS, TC])
        nmx = sb("nmx", [P, HEADS, TC])
        rs = sb("rs", [P, TC, HEADS])
        ri = sb("ri", [P, TC, HEADS])
        m8 = sb("m8", [P, TC, 8])
        room = sb("room", [P, TC])
        more = sb("more", [P, TC])
        nv0 = sb("nv0", [P, TC])
        den = sb("den", [P, TC])
        rden = sb("rden", [P, TC])
        npass = sb("npass", [E, 4])
        cum = sb("cum", [E, 2])
        ohA = sb("ohA", [E, TABLE])
        oh = sb("oh", [E, TABLE])
        ohz = sb("ohz", [E, TABLE])
        p64 = sb("p64", [P, TABLE])
        base = sb("base", [P, TABLE])
        slot_p = sb("slot_p", [P, TC, TABLE])
        gate_p = sb("gate_p", [P, TC, TABLE])
        tab = sb("tab", [1, TABLE + E], I32)

        q_flat = qT[:, :, :].rearrange("p k s -> p (k s)")
        n_bias = 2 * FC * TABLE
        bias_p = q_flat[:, 0:n_bias].rearrange("p (j m q) -> p j m q", j=2, m=FC)
        rT = q_flat[0:E, n_bias:n_bias + 2 * SEQ].rearrange("e (j s) -> e j s", j=2)

        at = n_bias + 2 * SEQ
        lg, gt, eq, sel, ew, ex, wt, rk, rkc = (
            q_flat[:, at + i * TC * E:at + (i + 1) * TC * E].rearrange("p (c e) -> p c e", c=TC) for i in range(9))
        at += 9 * TC * E
        n_scan = TC * (E + E // 2)
        scan = q_flat[:, at:at + 2 * n_scan].rearrange("p (b c e) -> p b c e", b=2, c=TC)

        wo_flat = wout[:, :, :].rearrange("p k n -> p (k n)")

        def temp(n, size, parts=P):
            return wo_flat[0:parts, n:n + size]

        xT = temp(0, 512).rearrange("p (k s) -> p k s", s=SLOTS)
        g1, g2, sg, gs = (temp(512 * i, 512) for i in (1, 2, 3, 4))
        u1, u2, act_t, yrows = (temp(512 * i, 512) for i in (5, 6, 7, 8))
        grow, urow = temp(512 * 9, 512), temp(512 * 10, 512)
        GT = temp(512 * 11, SEQ)
        S = temp(512 * 12, TC * SLOTS).rearrange("p (c s) -> p c s", s=SLOTS)
        G = temp(512 * 13, TC * 2 * SLOTS).rearrange("p (c s) -> p c s", s=2 * SLOTS)

        prob = work[:, 0:2, :].rearrange("p b (c k) -> p b c k", c=TC)
        probT = work[:, 2:4, :].rearrange("p b (c k) -> p b c k", c=TC)
        o = xs

        banks = [ctx.enter_context(nc.psum_tensor(f"bank{i}", [P, 512], F32)) for i in range(8)]

        ident = cst[:, C_ID:C_ID + P]
        tri = cst[:, C_TRI:C_TRI + P]
        tri_in = cst[0:E, C_TRI_IN:C_TRI_IN + E]
        ones = cst[:, C_ONE:C_ONE + P]
        iota = cst[:, C_IOTA:C_IOTA + SLOTS]
        iota_twice = cst[:, C_IOTA:C_IOTA + 2 * SLOTS]

        def table(at):
            return cst[:, at:at + TC * HD].rearrange("p (c d) -> p c d", c=TC)

        logm = cst[:, C_LOGM:C_END].rearrange("p (c k) -> p c k", c=TC)

        def unit(u):
            return ring[:, u * UNIT:(u + 1) * UNIT]

        x_in = [sem(f"x_in{c}") for c in range(TC)]
        cst_in = sem("cst_in")
        vecs_in = [sem(f"vecs_in{i}") for i in range(4)]
        qkg_in = [sem(f"qkg_in{i}") for i in range(2)]
        proj_in = [sem(f"proj_in{u}") for u in range(PROJ_UNITS)]
        wout_in = [sem(f"wout_in{i}") for i in range(4)]
        wr_in = sem("wr_in")
        brt_in = sem("brt_in")
        bg_in, bu_in, bd_in = sem("bg_in"), sem("bu_in"), sem("bd_in")
        fgain_in = sem("fgain_in")
        unit_in = [sem(f"unit_in{u}") for u in range(UNITS)]
        out_stored = sem("out_stored")
        sq_done = sem("sq_done")
        ms_done = sem("ms_done")
        rt_done = sem("rt_done")
        rstd_done = sem("rstd_done")
        xs_done = sem("xs_done")
        gains_turned, gains_ready = sem("gains_turned"), sem("gains_ready")
        rot_ready = sem("rot_ready")
        x_turned = sem("x_turned")
        hT_ready = sem("hT_ready")
        proj_done = sem("proj_done")
        hsq_done, hss_done = sem("hsq_done"), sem("hss_done")
        hms_done, hrt_done, hrs_done = sem("hms_done"), sem("hrt_done"), sem("hrs_done")
        normed = sem("normed")
        rot_parts = sem("rot_parts")
        rope_ready = sem("rope_ready")
        v_ready = sem("v_ready")
        qk_turned = sem("qk_turned")
        qkT_ready = sem("qkT_ready")
        scores_done = sem("scores_done")
        masked_ready = sem("masked_ready")
        mx_ready, nmx_ready = sem("mx_ready"), sem("nmx_ready")
        prob_ready = sem("prob_ready")
        prob_turned = sem("prob_turned")
        probTa_ready, probTb_ready = sem("probTa_ready"), sem("probTb_ready")
        pv_done = sem("pv_done")
        ri_ready = sem("ri_ready")
        o_ready = sem("o_ready")
        o_scaled = sem("o_scaled")
        oproj_done = sem("oproj_done")
        x1_ready = sem("x1_ready")
        logits_done = sem("logits_done")
        r_step = sem("r_step")
        exp_ready = sem("exp_ready")
        ranks_done, cum_done, turned_done = sem("ranks_done"), sem("cum_done"), sem("turned_done")
        picks_done, biases_done = sem("picks_done"), sem("biases_done")
        bdown_done = sem("bdown_done")
        biasg_ready, biasu_ready = sem("biasg_ready"), sem("biasu_ready")
        p64_ready = sem("p64_ready")
        tab_ready = sem("tab_ready")
        unit_used = [sem(f"unit_used{u}") for u in range(UNITS)]
        gathered, xT_ready = sem("gathered"), sem("xT_ready")
        S_ready, G_ready = sem("S_ready"), sem("G_ready")
        gate_biased, gate_clamped = sem("gate_biased"), sem("gate_clamped")
        sig_ready, gs_ready = sem("sig_ready"), sem("gs_ready")
        up_biased, up_clamped, act_ready = sem("up_biased"), sem("up_clamped"), sem("act_ready")
        grow_ready, urow_ready = sem("grow_ready"), sem("urow_ready")
        gate_turned, up_turned = sem("gate_turned"), sem("up_turned")
        G_turned, GT_ready = sem("G_turned"), sem("GT_ready")
        yrows_ready = sem("yrows_ready")
        spread = [sem(f"spread{i}") for i in range(4)]
        added = [sem(f"added{i}") for i in range(4)]
        fin_scaled = sem("fin_scaled")
        fin_ready = sem("fin_ready")

        block = ctx.enter_context(nc.Block())

        w_by_unit = [(w, 2 * j) for w in (w_gate, w_up, w_down) for j in range(4)]

        def load_unit(sp, u, e):
            w, k = w_by_unit[u]
            src = w[0, e, k * P:(k + 2) * P, :] if isinstance(e, int) else \
                w[0, bass.ds(e, 1), k * P:(k + 2) * P, :].rearrange("e r n -> (e r) n")
            sp.dma_start(unit(u).rearrange("p (k n) -> p k n", k=2),
                         src.rearrange("(k p) n -> p k n", p=P)).then_inc(unit_in[u], 16)

        @block.sync
        def _(sp):
            for c in range(TC):
                sp.dma_start(acc[:, c, :], x[0, c * P:(c + 1) * P, :]).then_inc(x_in[c], 16)
            sp.dma_start(cst[:, :], consts).then_inc(cst_in, 16)
            for _, col, width, u0 in PROJ:
                rows = UNIT // width
                for j in range(KC // rows):
                    sp.dma_start(
                        unit(u0 + j).rearrange("p (k n) -> p k n", n=width),
                        w_in[0, j * rows * P:(j + 1) * rows * P, col:col + width]
                        .rearrange("(k p) n -> p k n", p=P)).then_inc(proj_in[u0 + j], 16)
            for i in range(4):
                sp.dma_start(wout[:, 2 * i:2 * i + 2, :],
                             w_out[0, 2 * i * P:2 * (i + 1) * P, :]
                             .rearrange("(k p) n -> p k n", p=P)).then_inc(wout_in[i], 16)
            for u in range(PROJ_UNITS, UNITS):
                load_unit(sp, u, 0)
            for g, (_, _, width, u0) in enumerate(PROJ):
                sp.wait_ge(proj_done, 2 * g + 2)
                for j in range(KC * width // UNIT):
                    load_unit(sp, u0 + j, 0)
            sp.wait_ge(tab_ready, 1)
            with sp.Fori(1, E) as e:
                upto = sp.value_load(tab[0:1, bass.ds(e + (TABLE - 1), 1)],
                                     min_val=1, max_val=MAX_PASSES)
                for u in range(UNITS):
                    sp.wait_ge(unit_used[u], upto)
                    load_unit(sp, u, e)
            for c in range(TC):
                sp.wait_ge(fin_ready, c + 1)
                sp.dma_start(out[0, c * P:(c + 1) * P, :], xs[:, c, :]).then_inc(out_stored, 16)
            sp.wait_ge(out_stored, 16 * TC)

        @block.gpsimd
        def _(pool):
            pool.wait_ge(cst_in, 16)
            pool.tensor_scalar(p64[:, :], iota[:, 0:TABLE], float(SLOTS), 0.0, ALU.mult, ALU.add)\
                .then_inc(p64_ready, 1)

        @block.scalar
        def _(act):
            for i, (v, a, n) in enumerate(((attn_norm, 0, KC), (ffn_norm, KC, KC),
                                           (out_norm_a, 2 * KC, KC // 2),
                                           (out_norm_b, 2 * KC + KC // 2, KC // 2))):
                act.dma_start(vecs[a:a + n, :], v[0, :].rearrange("(k p) -> k p", p=P)).then_inc(vecs_in[i], 16)
            for i, v in enumerate((q_norm, k_norm)):
                act.dma_start(qkg[:, i, :], v.broadcast_to([P, HD])).then_inc(qkg_in[i], 16)

            def sum_squares(src, junk, col):
                act.activation(junk, src, ACT.Square, accum_out=ss[:, col:col + 1]).then_inc(sq_done, 1)

            def roots(n, a, b):
                act.wait_ge(ms_done, n)
                act.activation(rt[:, a:b], ms[:, a:b], ACT.Sqrt).then_inc(rt_done, 1)

            for c in range(TC):
                act.wait_ge(x_in[c], 16)
                sum_squares(acc[:, c, :], hT[:, 4 * c:4 * c + 4, :].rearrange("p k s -> p (k s)"), c)
                roots(c + 1, c, c + 1)
            act.dma_start(wr[:, :, :], w_router[0].rearrange("(k p) e -> p k e", p=P)).then_inc(wr_in, 16)
            act.dma_start(brt[:, :], b_router.broadcast_to([P, E])).then_inc(brt_in, 16)

            for i, heads in enumerate((HEADS_A, HEADS_A, KV_A, KV_A)):
                act.wait_ge(proj_done, i + 1)
                w = heads * HD
                if i >= 1:
                    act.wait_ge(hss_done, i)
                act.activation(work[:, 3, 0:w], banks[PROJ_BANK[i]][:, 0:w], ACT.Square).then_inc(hsq_done, 1)
                if i >= 2:
                    act.activation(vv[:, i % 2, 0:KV_A * HD], banks[PROJ_BANK[i]][:, w:2 * w], ACT.Copy).then_inc(v_ready, 1)
                act.wait_ge(hms_done, i + 1)
                act.activation(hrt[:, i, 0:heads], hms[:, i, 0:heads], ACT.Sqrt).then_inc(hrt_done, 1)
            for i in (4, 5):
                act.wait_ge(proj_done, i + 1)
                act.activation(vv[:, i % 2, KV_A * HD:], banks[PROJ_BANK[i]][:, :], ACT.Copy).then_inc(v_ready, 1)

            def qk_copy(n):
                dst, w, bank = ((qT[:, 0:2, :], 512, 2), (qT[:, 2:4, :], 512, 3), (kT[:, 0:1, :], 256, 4),
                                (qT[:, 4:6, :], 512, 1), (qT[:, 6:8, :], 512, 2),
                                (kT[:, 1:3, :], 512, 1), (kT[:, 3:5, :], 512, 2))[n]
                act.wait_ge(qk_turned, n + 1)
                act.activation(dst.rearrange("p k s -> p (k s)"), banks[bank][:, 0:w], ACT.Copy).then_inc(qkT_ready, 1)

            for n in range(5):
                qk_copy(n)

            def exps(h):
                b = h % 2
                act.wait_ge(nmx_ready, h + 1)
                if h >= 2:
                    act.wait_ge(prob_turned, h - 1)
                for c in range(TC):
                    src = banks[S_BANK[h % 3]][:, c * SEQ:(c + 1) * SEQ] if h < HEADS_A else masked[:, b, c, :]
                    last = act.activation(prob[:, b, c, :], src, ACT.Exp, bias=nmx[:, h, c:c + 1],
                                          scale=SCALE if h < HEADS_A else 1.0, accum_out=rs[:, c, h:h + 1])
                last.then_inc(prob_ready, 1)

            for i in range(HEADS + 3):
                if i < HEADS:
                    exps(i)
                if i == 1:
                    qk_copy(5)
                    qk_copy(6)
                    act.dma_start(bg, b_gate[0]).then_inc(bg_in, 16)
                    act.dma_start(bu, b_up[0]).then_inc(bu_in, 16)
                    act.dma_start(bd, b_down[0].rearrange("e (j n) -> e j n", j=2)).then_inc(bd_in, 16)
                if HEADS_A <= i - 2 < HEADS:
                    h = i - 2
                    act.wait_ge(prob_turned, h + 1)
                    act.wait_ge(pv_done, h - 1)
                    act.activation(probT[:, h % 2, :, :].rearrange("p c k -> p (c k)"), banks[PT_BANK[h % 2]][:, :],
                                   ACT.Copy).then_inc(probTb_ready, 1)

            act.wait_ge(scores_done, HEADS)
            act.dma_start(fgain, final_norm.rearrange("(a d) -> a d", a=1).broadcast_to([P, D])).then_inc(fgain_in, 16)

            for half in range(2):
                act.wait_ge(o_ready, 2 * half + 2)
                for c in range(TC):
                    sum_squares(o[:, c, half * 512:(half + 1) * 512], hT[:, 4 * half + 2 * c:4 * half + 2 * c + 2, :].rearrange("p k s -> p (k s)"), 2 + 2 * half + c)
            roots(3, 2, 6)
            for c in range(TC):
                act.wait_ge(x1_ready, 2 * c + 2)
                sum_squares(acc[:, c, :], qT[:, 4 * c:4 * c + 4, :].rearrange("p k s -> p (k s)"), 6 + c)
            roots(4, 6, 8)

            act.wait_ge(r_step, R_MAX)
            for c in range(TC):
                last = act.activation(ex[:, c, :], lg[:, c, :], ACT.Exp, bias=nv0[:, c:c + 1])
            last.then_inc(exp_ready, 1)
            act.wait_ge(biases_done, 2)
            act.activation(bias_p[:, 1, :, :].rearrange("p m q -> p (m q)"), banks[7][:, 0:FC * TABLE], ACT.Copy).then_inc(biasu_ready, 1)

            act.wait_ge(tab_ready, 1)
            passes = act.value_load(tab[0:1, TABLE + E - 1:TABLE + E], min_val=1, max_val=MAX_PASSES)

            def one_pass(p, first):
                act.wait_ge(unit_used[3], p + 1)
                if not first:
                    act.wait_ge(gate_turned, p)
                act.activation(grow, banks[1][:, :], ACT.Copy).then_inc(grow_ready, 1)
                act.wait_ge(gate_clamped, p + 1)
                act.activation(sg, g2, ACT.Sigmoid, scale=ALPHA).then_inc(sig_ready, 1)
                if not first:
                    turned_slots(p)
                act.wait_ge(unit_used[7], p + 1)
                act.activation(urow, banks[2][:, :], ACT.Copy).then_inc(urow_ready, 1)
                act.wait_ge(unit_used[UNITS - 1], p + 1)
                act.activation(yrows, banks[3][:, :], ACT.Copy).then_inc(yrows_ready, 1)

            def turned_slots(p):
                act.wait_ge(G_turned, p)
                act.activation(GT, banks[6][:, 0:SEQ], ACT.Copy).then_inc(GT_ready, 1)

            one_pass(0, True)
            with act.Fori(1, passes) as p:
                one_pass(p, False)
            turned_slots(passes)

            for c in range(TC):
                act.wait_ge(added[2 * c], passes + 1)
                act.wait_ge(added[2 * c + 1], passes + 1)
                sum_squares(acc[:, c, :], wo_flat[:, c * D:(c + 1) * D], 8 + c)
            roots(5, 8, 10)

        @block.tensor
        def _(pe):
            pe.wait_ge(cst_in, 16)
            for i in range(4):
                pe.wait_ge(vecs_in[i], 16)
            pe.transpose(banks[7][:, 0:3 * KC], vecs[:, :], ident[0:3 * KC, 0:3 * KC]).then_inc(gains_turned, 1)

            def turn_rows(src, bank0):
                for j in range(KC // 2):
                    for kk in range(2):
                        for c in range(TC):
                            k = 2 * j + kk
                            last = pe.transpose(banks[bank0 + j][:, kk * SEQ + c * P:kk * SEQ + (c + 1) * P],
                                                src[:, c, k * P:(k + 1) * P], ident)
                    last.then_inc(x_turned, 1)

            pe.wait_ge(xs_done, TC)
            turn_rows(xs, 0)

            def project(g):
                _, _, width, u0 = PROJ[g]
                rows = UNIT // width
                for c in range(TC):
                    i = 2 * g + c
                    if i == 6:
                        pe.wait_ge(rope_ready, 2)
                    if i == 7 or i == 8:
                        pe.wait_ge(rope_ready, i - 4)
                        pe.wait_ge(v_ready, i - 6)
                    if i == 9:
                        pe.wait_ge(v_ready, 3)
                    for k in range(KC):
                        pe.wait_ge(proj_in[u0 + k // rows], 16)
                        pe.wait_ge(hT_ready, k // 2 + 1)
                        if i == 3 and k == 0:
                            pe.wait_ge(gains_ready, 1)
                        last = pe.matmul(banks[PROJ_BANK[i]][:, 0:width], hT[:, k, c * P:(c + 1) * P],
                                         unit(u0 + k // rows)[:, (k % rows) * width:(k % rows + 1) * width],
                                         start=(k == 0), stop=(k == KC - 1))
                    last.then_inc(proj_done, 1)

            def turn_pairs(src, pairs, bank):
                for n, pair in enumerate(pairs):
                    for c in range(TC):
                        last = pe.transpose(banks[bank][:, n * SEQ + c * P:n * SEQ + (c + 1) * P],
                                            src[:, c, pair * P:(pair + 1) * P], ident)
                last.then_inc(qk_turned, 1)

            project(0)
            project(1)
            project(2)
            pe.wait_ge(rope_ready, 4)
            turn_pairs(qr, (0, 1), 2)
            turn_pairs(qr, (2, 3), 3)
            turn_pairs(kr, (0,), 4)
            project(3)
            project(4)
            pe.wait_ge(rope_ready, 6)
            pe.wait_ge(v_ready, 4)
            turn_pairs(qr, (4, 5), 1)
            pe.wait_ge(qkT_ready, 1)
            turn_pairs(qr, (6, 7), 2)

            def scores(h):
                if h < HEADS_A:
                    row, pair, kpair = (h // GROUP_A) * HD, h % GROUP_A, 0
                    pe.wait_ge(qkT_ready, 3)
                else:
                    row, pair = (h % 2) * HD, h // 2
                    kpair = 1 + (h - HEADS_A) // 2
                    pe.wait_ge(qkT_ready, 7)
                if h == 2:
                    pe.wait_ge(qkT_ready, 7)
                if h >= 3:
                    pe.wait_ge(prob_ready, h - 2)
                for c in range(TC):
                    last = pe.matmul(banks[S_BANK[h % 3]][:, c * SEQ:(c + 1) * SEQ],
                                     qT[row:row + HD, pair, c * P:(c + 1) * P], kT[row:row + HD, kpair, :],
                                     start=True, stop=True)
                last.then_inc(scores_done, 1)

            def turn_probs(h):
                pe.wait_ge(prob_ready, h + 1)
                if h < 2:
                    pe.wait_ge(rope_ready, 5 + h)
                else:
                    wait_probT(h - 2)
                for kc in range(TC):
                    for c in range(TC):
                        last = pe.transpose(banks[PT_BANK[h % 2]][:, kc * SEQ + c * P:kc * SEQ + (c + 1) * P],
                                            prob[:, h % 2, c, kc * P:(kc + 1) * P], ident)
                last.then_inc(prob_turned, 1)

            def wait_probT(h):
                if h < HEADS_A:
                    pe.wait_ge(probTa_ready, h + 1)
                else:
                    pe.wait_ge(probTb_ready, h - HEADS_A + 1)

            def weigh_values(h):
                wait_probT(h)
                bank = O_BANK[(h // 4) % 2]
                if h < 8 and h % 4 == 0:
                    pe.wait_ge(rope_ready, 7 + h // 4)
                if h >= 8 and h % 4 == 0:
                    pe.wait_ge(o_ready, h // 4 - 1)
                vh = h // GROUP_A if h < HEADS_A else KV_A + h - HEADS_A
                for c in range(TC):
                    for kc in range(TC):
                        last = pe.matmul(banks[bank][:, c * 256 + (h % 4) * HD:c * 256 + (h % 4 + 1) * HD],
                                         probT[:, h % 2, kc, c * P:(c + 1) * P], vv[:, kc, vh * HD:(vh + 1) * HD],
                                         start=(kc == 0), stop=(kc == TC - 1))
                last.then_inc(pv_done, 1)

            for i in range(HEADS + 3):
                if i < HEADS:
                    scores(i)
                if i == 1:
                    pe.wait_ge(rope_ready, 8)
                    pe.wait_ge(qkT_ready, 5)
                    turn_pairs(kr, (1, 2), 1)
                    turn_pairs(kr, (3, 4), 2)
                if 0 <= i - 2 < HEADS:
                    turn_probs(i - 2)
                if 0 <= i - 3 < HEADS:
                    weigh_values(i - 3)

            pe.wait_ge(o_scaled, 2 * TC)
            turn_rows(o, 1)
            for c in range(TC):
                for n in range(2):
                    for k in range(KC):
                        pe.wait_ge(hT_ready, 4 + k // 2 + 1)
                        pe.wait_ge(wout_in[k // 2], 16)
                        last = pe.matmul(banks[OP_BANK[2 * c + n]][:, :], hT[:, k, c * P:(c + 1) * P],
                                         wout[:, k, n * 512:(n + 1) * 512], start=(k == 0), stop=(k == KC - 1))
                    last.then_inc(oproj_done, 1)

            pe.wait_ge(xs_done, 2 * TC)
            turn_rows(xs, 1)
            pe.wait_ge(wr_in, 16)
            for c in range(TC):
                for k in range(KC):
                    pe.wait_ge(hT_ready, 8 + k // 2 + 1)
                    last = pe.matmul(banks[5][:, c * E:(c + 1) * E], hT[:, k, c * P:(c + 1) * P], wr[:, k, :],
                                     start=(k == 0), stop=(k == KC - 1))
            last.then_inc(logits_done, 1)
            pe.wait_ge(r_step, R_SEL)
            pe.matmul(banks[6][:, 0:E], tri, sel[:, 0, :], start=True, stop=True)
            pe.matmul(banks[6][:, E:2 * E], tri, sel[:, 1, :], start=True, stop=False)
            pe.matmul(banks[6][:, E:2 * E], ones, sel[:, 0, :], start=False, stop=True)
            pe.matmul(banks[6][0:E, 2 * E:2 * E + 1], sel[:, 0, :], ones[:, 0:1], start=True, stop=False)
            pe.matmul(banks[6][0:E, 2 * E:2 * E + 1], sel[:, 1, :], ones[:, 0:1], start=False, stop=True)\
              .then_inc(ranks_done, 1)
            pe.wait_ge(r_step, R_NPASS)
            pe.matmul(banks[0][0:E, 0:1], tri_in, npass[:, 3:4], start=True, stop=True).then_inc(cum_done, 1)
            pe.wait_ge(r_step, R_WT)
            for c in range(TC):
                pe.transpose(banks[1][0:E, c * P:(c + 1) * P], rkc[:, c, :], ident)
                last = pe.transpose(banks[1][0:E, SEQ + c * P:SEQ + (c + 1) * P], wt[:, c, :], ident)
            last.then_inc(turned_done, 1)
            pe.wait_ge(r_step, R_PICK)
            pe.matmul(banks[2][0:1, 0:TABLE], ones[0:E, 0:1], ohA[:, :], start=True, stop=True)
            pe.matmul(banks[2][0:1, TABLE:TABLE + E], cum[:, 0:1], ident[0:E, 0:E], start=True, stop=True)
            pe.matmul(banks[2][:, 128:128 + TABLE], ones[0:E, :], ohz[:, :], start=True, stop=True)
            for c in range(TC):
                for j in range(2):
                    at = 192 + (2 * j + c) * TABLE
                    last = pe.matmul(banks[2][:, at:at + TABLE], rT[:, j, c * P:(c + 1) * P], oh[:, :],
                                     start=True, stop=True)
            last.then_inc(picks_done, 1)
            pe.wait_ge(bg_in, 16)
            pe.wait_ge(bu_in, 16)
            for j, b in enumerate((bg, bu)):
                for m in range(FC):
                    last = pe.matmul(banks[3 if j == 0 else 7][:, m * TABLE:(m + 1) * TABLE],
                                     b[:, m * P:(m + 1) * P], oh[:, :], start=True, stop=True)
                last.then_inc(biases_done, 1)
            pe.wait_ge(bd_in, 16)
            pe.wait_ge(r_step, R_PSUM)
            for c in range(TC):
                for n in range(2):
                    if 2 * c + n == 0:
                        pe.wait_ge(biasu_ready, 1)
                        pe.wait_ge(biasg_ready, 1)
                    pe.matmul(banks[SP_BANK[2 * c + n]][:, :], rT[:, 1, c * P:(c + 1) * P], bd[:, n, :],
                              start=True, stop=True).then_inc(bdown_done, 1)

            pe.wait_ge(tab_ready, 1)
            passes = pe.value_load(tab[0:1, TABLE + E - 1:TABLE + E], min_val=1, max_val=MAX_PASSES)

            def gather(n_ready):
                pe.wait_ge(S_ready, n_ready)
                for k in range(KC):
                    for c in range(TC):
                        last = pe.matmul(banks[0][:, k * SLOTS:(k + 1) * SLOTS], xs[:, c, k * P:(k + 1) * P],
                                         S[:, c, :], start=(c == 0), stop=(c == TC - 1))
                last.then_inc(gathered, 1)

            def product(bank, src, units, landed):
                for u in units:
                    pe.wait_ge(unit_in[u], landed)
                    for kk in range(2):
                        k = 2 * (u % 4) + kk
                        for half in range(2):
                            last = pe.matmul(banks[bank][half * SLOTS:(half + 1) * SLOTS, :], src(k),
                                             unit(u)[:, kk * F + half * 512:kk * F + (half + 1) * 512],
                                             start=(k == 0), stop=(k == KC - 1))
                    last.then_inc(unit_used[u], 1)

            def turn(bank, src, done):
                for m in range(FC // 2):
                    last = pe.transpose(banks[bank][:, m * P:(m + 1) * P], src[:, m * P:(m + 1) * P], ident)
                last.then_inc(done, 1)

            def turn_slots(p):
                pe.wait_ge(added[1], p)
                pe.wait_ge(G_ready, p)
                for c in range(TC):
                    last = pe.transpose(banks[6][:, c * P:(c + 1) * P], G[:, c, :], ident)
                last.then_inc(G_turned, 1)

            def spread_results(p, bank4_read):
                pe.wait_ge(GT_ready, p)
                pe.wait_ge(yrows_ready, p)
                pe.wait_ge(added[0], p)
                for i in range(4):
                    c, n = i // 2, i % 2
                    if i == 3:
                        pe.wait_ge(gate_biased, bank4_read)
                    half = slice(n * SLOTS, (n + 1) * SLOTS)
                    pe.matmul(banks[SP_BANK[i]][:, :], GT[half, c * P:(c + 1) * P], yrows[half, :],
                              start=True, stop=True).then_inc(spread[i], 1)

            def one_pass(p, first):
                expert = pe.value_load(tab[0:1, bass.ds(p, 1)], min_val=0, max_val=E)
                landed = 16 if first else pe.snap(expert * 16 + 16)
                pe.wait_ge(xT_ready, p + 1)
                if not first:
                    pe.wait_ge(grow_ready, p)
                product(1, lambda k: xT[:, k, :], range(0, 4), landed)
                if not first:
                    turn_slots(p)
                    pe.wait_ge(urow_ready, p)
                product(2, lambda k: xT[:, k, :], range(4, 6), landed)
                pe.wait_ge(grow_ready, p + 1)
                pe.wait_ge(added[3], 1 if first else p)
                turn(4, grow, gate_turned)
                product(2, lambda k: xT[:, k, :], range(6, 8), landed)
                if not first:
                    spread_results(p, p + 1)
                    pe.wait_ge(up_biased, p)
                pe.wait_ge(urow_ready, p + 1)
                turn(5, urow, up_turned)
                gather(p + 2)
                pe.wait_ge(act_ready, p + 1)
                pe.wait_ge(added[2], p + 1)
                product(3, lambda k: act_t[:, act_at(k):act_at(k) + SLOTS], range(8, 12), landed)

            def act_at(k):
                return (k % 4) * 2 * SLOTS + (k // 4) * SLOTS

            gather(1)
            one_pass(0, True)
            with pe.Fori(1, passes) as p:
                one_pass(p, False)
            turn_slots(passes)
            spread_results(passes, passes)

        @block.vector
        def _(dve):
            def means(n_sq, n, a, b, width):
                dve.wait_ge(sq_done, n_sq)
                dve.tensor_scalar(ms[:, a:b], ss[:, a:b], 1.0 / width, EPS, ALU.mult, ALU.add).then_inc(ms_done, 1)
                dve.wait_ge(rt_done, n)
                dve.reciprocal(rstd[:, a:b], rt[:, a:b]).then_inc(rstd_done, 1)
                dve.wait_ge(rstd_done, n)

            for c in range(TC):
                dve.wait_ge(x_in[c], 16)
                means(c + 1, c + 1, c, c + 1, D)
                dve.tensor_scalar(xs[:, c, :], acc[:, c, :], rstd[:, c:c + 1], None, ALU.mult).then_inc(xs_done, 1)

            dve.wait_ge(gains_turned, 1)
            dve.tensor_copy(gains[:, :], banks[7][:, 0:3 * KC]).then_inc(gains_ready, 1)
            dve.wait_ge(gains_ready, 1)

            def scaled_rows(rounds, bank0, col):
                for j in range(KC // 2):
                    dve.wait_ge(x_turned, 4 * rounds + j + 1)
                    g = gains[:, col + 2 * j:col + 2 * j + 2].unsqueeze(2).broadcast_to([P, 2, SEQ])
                    dve.tensor_tensor(hT[:, 2 * j:2 * j + 2, :],
                                      banks[bank0 + j][:, :].rearrange("p (k s) -> p k s", k=2), g, ALU.mult)\
                       .then_inc(hT_ready, 1)

            scaled_rows(0, 0, 0)

            dve.wait_ge(cst_in, 16)
            for i in range(2):
                dve.wait_ge(qkg_in[i], 16)
                for c in range(TC):
                    dve.tensor_tensor(rot[:, i, 0, c, :], table(C_COSA)[:, c, :], qkg[:, i, :], ALU.mult)
                    for a, b in ((0, 16), (16, 0), (32, 48), (48, 32)):
                        last = dve.tensor_tensor(rot[:, i, 1, c, a:a + 16], table(C_SINA)[:, c, a:a + 16],
                                                 qkg[:, i, b:b + 16], ALU.mult)
            last.then_inc(rot_ready, 1)
            dve.wait_ge(rot_ready, 1)

            def bc(t, heads):
                return t.unsqueeze(1).broadcast_to([P, heads, t.shape[-1]])

            n_rope = 0

            def rotate(src, dst, view, heads, half, cos, sin):
                nonlocal n_rope
                n_rope += 1
                w = heads * HD
                t1, t2 = work[:, 0, 0:w], work[:, 1, 0:w]
                if n_rope > 1:
                    dve.wait_ge(rope_ready, n_rope - 1)
                dve.tensor_tensor(t1.rearrange("p (h d) -> p h d", d=HD), src.rearrange("p (h d) -> p h d", d=HD),
                                  bc(cos, heads), ALU.mult)
                for at in range(0, HD, half):
                    other = at + half if at // half % 2 == 0 else at - half
                    last = dve.tensor_tensor(
                        t2.rearrange("p (h d) -> p h d", d=HD)[:, :, at:at + half],
                        src.rearrange("p (h d) -> p h d", d=HD)[:, :, other:other + half],
                        bc(sin[:, at:at + half], heads), ALU.mult)
                last.then_inc(rot_parts, 1)
                dve.wait_ge(rot_parts, n_rope)
                dve.tensor_tensor(dst, view(t1), view(t2), ALU.add).then_inc(rope_ready, 1)

            def by_head(t):
                return t.rearrange("p (h d) -> p h d", d=HD)

            def by_pair(t):
                return t.rearrange("p (two j d) -> p two j d", two=2, d=HD)

            for i, heads in enumerate((HEADS_A, HEADS_A, KV_A, KV_A)):
                c, is_k = i % 2, i // 2
                w = heads * HD
                dve.wait_ge(hsq_done, i + 1)
                dve.tensor_reduce(hss[:, i, 0:heads], by_head(work[:, 3, 0:w]), AX.X, ALU.add).then_inc(hss_done, 1)
                dve.wait_ge(hss_done, i + 1)
                dve.tensor_scalar(hms[:, i, 0:heads], hss[:, i, 0:heads], 1.0 / HD, EPS, ALU.mult, ALU.add)\
                   .then_inc(hms_done, 1)
                dve.wait_ge(hrt_done, i + 1)
                dve.reciprocal(hrs[:, i, 0:heads], hrt[:, i, 0:heads]).then_inc(hrs_done, 1)
                dve.wait_ge(hrs_done, i + 1)
                t0 = work[:, 2, 0:w]
                dve.tensor_tensor(by_head(t0), by_head(banks[PROJ_BANK[i]][:, 0:w]),
                                  hrs[:, i, 0:heads].unsqueeze(2).broadcast_to([P, heads, HD]), ALU.mult)\
                   .then_inc(normed, 1)
                dve.wait_ge(normed, i + 1)
                if is_k:
                    rotate(t0, by_head(kr[:, c, 0:w]), by_head, heads, 16, rot[:, 1, 0, c, :], rot[:, 1, 1, c, :])
                else:
                    dst = qr[:, c, 0:w].rearrange("p (j two d) -> p two j d", two=2, d=HD)
                    rotate(t0, dst, by_pair, heads, 16, rot[:, 0, 0, c, :], rot[:, 0, 1, c, :])
            for i in range(6, 10):
                c = i % 2
                dve.wait_ge(proj_done, i + 1)
                dst = qr[:, c, HEADS_A * HD:] if i < 8 else kr[:, c, KV_A * HD:]
                rotate(banks[PROJ_BANK[i]][:, :], by_head(dst), by_head, HEADS_B, 32,
                       table(C_COSB)[:, c, :], table(C_SINB)[:, c, :])

            def row_max(h):
                dve.wait_ge(scores_done, h + 1)
                src = banks[S_BANK[h % 3]][:, :].rearrange("p (c k) -> p c k", c=TC)
                if h < HEADS_A:
                    dve.tensor_reduce(mx[:, h, :], src, AX.X, ALU.max).then_inc(mx_ready, 1)
                    dve.wait_ge(mx_ready, h + 1)
                    dve.tensor_scalar(nmx[:, h, :], mx[:, h, :], -SCALE, None, ALU.mult).then_inc(nmx_ready, 1)
                else:
                    dve.wait_ge(prob_ready, h - 1)
                    dve.scalar_tensor_tensor(out=masked[:, h % 2, :, :], in0=src, scalar=SCALE, in1=logm,
                                             op0=ALU.mult, op1=ALU.add).then_inc(masked_ready, 1)
                    dve.wait_ge(masked_ready, h - HEADS_A + 1)
                    dve.tensor_reduce(nmx[:, h, :], masked[:, h % 2, :, :], AX.X, ALU.max, negate=True)\
                       .then_inc(nmx_ready, 1)

            for i in range(HEADS + 3):
                if i < HEADS:
                    row_max(i)
                if 0 <= i - 2 < HEADS_A:
                    h = i - 2
                    dve.wait_ge(prob_turned, h + 1)
                    if h >= 2:
                        dve.wait_ge(pv_done, h - 1)
                    dve.tensor_copy(probT[:, h % 2, :, :].rearrange("p c k -> p (c k)"), banks[PT_BANK[h % 2]][:, :])\
                       .then_inc(probTa_ready, 1)
                if i >= 3 and (i - 3) % 4 == 3:
                    n = (i - 3) // 4
                    heads = slice(4 * n, 4 * n + 4)
                    dve.wait_ge(prob_ready, 4 * n + 4)
                    dve.reciprocal(ri[:, :, heads], rs[:, :, heads]).then_inc(ri_ready, 1)
                    dve.wait_ge(ri_ready, n + 1)
                    dve.wait_ge(pv_done, 4 * n + 4)
                    for c in range(TC):
                        last = dve.tensor_tensor(by_head(o[:, c, 256 * n:256 * (n + 1)]),
                                                 by_head(banks[O_BANK[n % 2]][:, c * 256:(c + 1) * 256]),
                                                 ri[:, c, heads].unsqueeze(2).broadcast_to([P, 4, HD]), ALU.mult)
                    last.then_inc(o_ready, 1)

            means(6, 3, 2, 6, 512)
            for half in range(2):
                for c in range(TC):
                    part = o[:, c, half * 512:(half + 1) * 512]
                    dve.tensor_scalar(part, part, rstd[:, 2 + 2 * half + c:3 + 2 * half + c], None, ALU.mult)\
                       .then_inc(o_scaled, 1)
            scaled_rows(1, 1, 2 * KC)
            for i in range(4):
                c, n = i // 2, i % 2
                part = acc[:, c, n * 512:(n + 1) * 512]
                dve.wait_ge(oproj_done, i + 1)
                dve.tensor_tensor(part, banks[OP_BANK[i]][:, :], part, ALU.add).then_inc(x1_ready, 1)
            means(8, 4, 6, 8, D)
            for c in range(TC):
                dve.tensor_scalar(xs[:, c, :], acc[:, c, :], rstd[:, 6 + c:7 + c], None, ALU.mult).then_inc(xs_done, 1)
            scaled_rows(2, 1, KC)

            n_step = 0

            def step(ins):
                nonlocal n_step
                n_step += 1
                ins.then_inc(r_step, 1)
                dve.wait_ge(r_step, n_step)

            for b in range(2):
                dve.memset(scan[:, b, :, 0:E // 2], 0.0)
            dve.wait_ge(logits_done, 1)
            dve.wait_ge(brt_in, 16)
            step(dve.tensor_tensor(lg[:, :, :], banks[5][:, 0:TC * E].rearrange("p (c e) -> p c e", c=TC),
                                   brt[:, :].unsqueeze(1).broadcast_to([P, TC, E]), ALU.add))
            for c in range(TC):
                last = dve.max(m8[:, c, :], lg[:, c, :])
            step(last)
            step(dve.tensor_scalar(nv0[:, :], m8[:, :, 0], -1.0, None, ALU.mult))
            assert n_step == R_MAX
            kth = m8[:, :, TOP_K - 1:TOP_K].broadcast_to([P, TC, E])
            pad = E // 2
            dve.tensor_tensor(gt[:, :, :], lg[:, :, :], kth, ALU.is_gt)
            dve.tensor_tensor(eq[:, :, :], lg[:, :, :], kth, ALU.is_equal)
            step(dve.tensor_tensor(scan[:, 0, :, pad:], lg[:, :, :], kth, ALU.is_equal))
            step(dve.tensor_reduce(more[:, :], gt[:, :, :], AX.X, ALU.add))
            step(dve.tensor_scalar(room[:, :], more[:, :], -1.0, float(TOP_K), ALU.mult, ALU.add))
            b = 0
            for shift in (1, 2, 4, 8, 16):
                step(dve.tensor_tensor(scan[:, 1 - b, :, pad:], scan[:, b, :, pad:],
                                       scan[:, b, :, pad - shift:pad + E - shift], ALU.add))
                b = 1 - b
            step(dve.tensor_tensor(ew[:, :, :], scan[:, b, :, pad:], room[:, :].unsqueeze(2).broadcast_to([P, TC, E]),
                                   ALU.is_le))
            step(dve.tensor_tensor(ew[:, :, :], ew[:, :, :], eq[:, :, :], ALU.mult))
            step(dve.tensor_tensor(sel[:, :, :], ew[:, :, :], gt[:, :, :], ALU.add))
            assert n_step == R_SEL
            dve.wait_ge(exp_ready, 1)
            step(dve.tensor_tensor(ew[:, :, :], ex[:, :, :], sel[:, :, :], ALU.mult))
            step(dve.tensor_reduce(den[:, :], ew[:, :, :], AX.X, ALU.add))
            step(dve.reciprocal(rden[:, :], den[:, :]))
            step(dve.tensor_tensor(wt[:, :, :], ew[:, :, :], rden[:, :].unsqueeze(2).broadcast_to([P, TC, E]), ALU.mult))
            dve.wait_ge(ranks_done, 1)
            count = banks[6][0:E, 2 * E:2 * E + 1]
            dve.tensor_scalar(npass[:, 0:1], count, float(SLOTS), 1.0, ALU.is_gt, ALU.add)
            dve.tensor_scalar(npass[:, 1:2], count, float(2 * SLOTS), None, ALU.is_gt)
            step(dve.tensor_scalar(npass[:, 2:3], count, float(3 * SLOTS), None, ALU.is_gt))
            step(dve.tensor_reduce(npass[:, 3:4], npass[:, 0:3], AX.X, ALU.add))
            assert n_step == R_NPASS
            step(dve.scalar_tensor_tensor(out=rk[:, :, :], in0=banks[6][:, 0:TC * E].rearrange("p (c e) -> p c e", c=TC),
                                          scalar=-NOT_ROUTED, in1=sel[:, :, :], op0=ALU.add, op1=ALU.mult))
            step(dve.tensor_scalar(rkc[:, :, :], rk[:, :, :], NOT_ROUTED, None, ALU.add))
            assert n_step == R_WT
            dve.wait_ge(cum_done, 1)
            step(dve.tensor_copy(cum[:, 0:1], banks[0][0:E, 0:1]))
            step(dve.tensor_tensor(cum[:, 1:2], cum[:, 0:1], npass[:, 3:4], ALU.subtract))
            numbers = iota[0:E, 0:TABLE]
            step(dve.tensor_scalar(ohA[:, :], numbers, cum[:, 0:1], None, ALU.is_ge))
            step(dve.scalar_tensor_tensor(out=oh[:, :], in0=numbers, scalar=cum[:, 1:2], in1=ohA[:, :],
                                          op0=ALU.is_ge, op1=ALU.subtract))
            step(dve.tensor_scalar(ohz[:, :], oh[:, :], cum[:, 1:2], None, ALU.mult))
            dve.wait_ge(turned_done, 1)
            step(dve.tensor_copy(rT[:, :, :].rearrange("e j s -> e (j s)"), banks[1][0:E, :]))
            assert n_step == R_PICK
            dve.wait_ge(picks_done, 1)
            dve.tensor_copy(tab[:, :], banks[2][0:1, 0:TABLE + E]).then_inc(tab_ready, 1)
            dve.wait_ge(p64_ready, 1)
            step(dve.scalar_tensor_tensor(out=base[:, :], in0=banks[2][:, 128:128 + TABLE], scalar=float(SLOTS),
                                          in1=p64[:, :], op0=ALU.mult, op1=ALU.subtract))
            pick = banks[2][:, 192:192 + 4 * TABLE].rearrange("p (j c q) -> p j c q", j=2, c=TC)
            step(dve.tensor_tensor(slot_p[:, :, :], pick[:, 0], base[:, :].unsqueeze(1).broadcast_to([P, TC, TABLE]),
                                   ALU.add))
            step(dve.tensor_copy(gate_p[:, :, :], pick[:, 1]))
            assert n_step == R_PSUM

            def slots_of(p):
                for c in range(TC):
                    last = dve.tensor_scalar(S[:, c, :], iota, slot_p[:, c, bass.ds(p, 1)], None, ALU.is_equal)
                last.then_inc(S_ready, 1)

            def gated_slots_of(p):
                for c in range(TC):
                    last = dve.tensor_scalar(G[:, c, :], iota_twice, slot_p[:, c, bass.ds(p, 1)],
                                             gate_p[:, c, bass.ds(p, 1)], ALU.is_equal, ALU.mult)
                last.then_inc(G_ready, 1)

            ffn_gain = gains[:, KC:2 * KC].unsqueeze(2).broadcast_to([P, KC, SLOTS])

            def tokens_out(n):
                dve.wait_ge(gathered, n)
                dve.tensor_tensor(xT, banks[0][:, :].rearrange("p (k s) -> p k s", k=KC), ffn_gain, ALU.mult)\
                   .then_inc(xT_ready, 1)

            def with_bias(dst, bank, j, p):
                for half in range(2):
                    b = bias_p[:, j, half * 4:half * 4 + 4, bass.ds(p, 1)].broadcast_to([P, FC // 2, SLOTS])

                    def part(t):
                        return t.rearrange("p (m h s) -> p h m s", m=FC // 2, h=2)[:, half]
                    last = dve.tensor_tensor(part(dst), part(banks[bank][:, :]), b, ALU.add)
                return last

            def add_up(p):
                for i in range(4):
                    c, n = i // 2, i % 2
                    part = acc[:, c, n * 512:(n + 1) * 512]
                    dve.wait_ge(spread[i], p)
                    dve.wait_ge(added[i], p)
                    dve.tensor_tensor(part, banks[SP_BANK[i]][:, :], part, ALU.add).then_inc(added[i], 1)

            slots_of(0)
            dve.wait_ge(biases_done, 1)
            dve.tensor_copy(bias_p[:, 0, :, :].rearrange("p m q -> p (m q)"), banks[3][:, 0:FC * TABLE])\
               .then_inc(biasg_ready, 1)
            for i in range(4):
                c, n = i // 2, i % 2
                part = acc[:, c, n * 512:(n + 1) * 512]
                dve.wait_ge(bdown_done, i + 1)
                dve.tensor_tensor(part, banks[SP_BANK[i]][:, :], part, ALU.add).then_inc(added[i], 1)
            tokens_out(1)
            dve.wait_ge(biasg_ready, 1)
            dve.wait_ge(biasu_ready, 1)

            def one_pass(p, first):
                dve.wait_ge(gate_turned, p + 1)
                with_bias(g1, 4, 0, p).then_inc(gate_biased, 1)
                dve.wait_ge(gate_biased, p + 1)
                dve.tensor_scalar(g2, g1, LIMIT, None, ALU.min).then_inc(gate_clamped, 1)
                dve.wait_ge(gathered, p + 1)
                slots_of(p + 1)
                dve.wait_ge(gate_clamped, p + 1)
                dve.wait_ge(sig_ready, p + 1)
                dve.tensor_tensor(gs, g2, sg, ALU.mult).then_inc(gs_ready, 1)
                if not first:
                    add_up(p)
                dve.wait_ge(up_turned, p + 1)
                with_bias(u1, 5, 1, p).then_inc(up_biased, 1)
                dve.wait_ge(up_biased, p + 1)
                dve.tensor_scalar(u2, u1, -LIMIT, LIMIT, ALU.max, ALU.min).then_inc(up_clamped, 1)
                dve.wait_ge(up_clamped, p + 1)
                dve.wait_ge(gs_ready, p + 1)
                if not first:
                    dve.wait_ge(unit_used[UNITS - 1], p)
                dve.scalar_tensor_tensor(out=act_t, in0=u2, scalar=1.0, in1=gs, op0=ALU.add, op1=ALU.mult)\
                   .then_inc(act_ready, 1)
                tokens_out(p + 2)
                if not first:
                    dve.wait_ge(G_turned, p)
                gated_slots_of(p)

            dve.wait_ge(tab_ready, 1)
            passes = dve.value_load(tab[0:1, TABLE + E - 1:TABLE + E], min_val=1, max_val=MAX_PASSES)
            one_pass(0, True)
            with dve.Fori(1, passes) as p:
                one_pass(p, False)
            add_up(passes)

            means(10, 5, 8, 10, D)
            dve.wait_ge(fgain_in, 16)
            for c in range(TC):
                dve.tensor_scalar(xs[:, c, :], acc[:, c, :], rstd[:, 8 + c:9 + c], None, ALU.mult).then_inc(fin_scaled, 1)
                dve.wait_ge(fin_scaled, c + 1)
                dve.tensor_tensor(xs[:, c, :], xs[:, c, :], fgain[:, :], ALU.mult).then_inc(fin_ready, 1)


INS = ("x", "attn_norm", "w_in", "q_norm", "k_norm", "out_norm_a", "out_norm_b", "w_out", "ffn_norm",
       "w_router", "b_router", "w_gate", "b_gate", "w_up", "b_up", "w_down", "b_down", "final_norm")


def kernel(**inputs):
    import concourse.bacc as bacc
    from concourse.bass_utils import run_bass_kernel_spmd

    nc = bacc.Bacc("TRN2", target_bir_lowering=False, num_devices=1)
    arrays, args = {}, []
    for name in INS:
        arrays[name] = np.ascontiguousarray(inputs[name])
    arrays["consts"] = constants()
    for name, a in arrays.items():
        args.append(nc.dram_tensor(name, a.shape, F32, kind="ExternalInput").ap())
    out = nc.dram_tensor("out", arrays["x"].shape, F32, kind="ExternalOutput").ap()
    encoder_kernel(nc, *args, out)
    r = run_bass_kernel_spmd(nc, [arrays], core_ids=[0])
    return r.results[0]["out"]
```

```python
from contextlib import ExitStack

import concourse.bass as bass
import numpy as np
from concourse import mybir

ALU = mybir.AluOpType
ACT = mybir.ActivationFunctionType
AX = mybir.AxisListType
F32 = mybir.dt.float32
I32 = mybir.dt.int32

P = 128
SEQ = 256
D = 1024
TC = SEQ // P
KC = D // P
HD = 64
HEADS_A, KV_A, HEADS_B = 8, 2, 8
HEADS = HEADS_A + HEADS_B
GROUP_A = HEADS_A // KV_A
BRANCHES = ((128, 1), (512, 4), (2048, 16))
GRID_W = 64
THETA = 10000.0
E = 32
TOP_K = 4
F = 1024
FC = F // P
LIMIT = 7.0
ALPHA = 1.702
EPS = 1e-6
SCALE = HD ** -0.5

SLOTS = 64
MAX_PASSES = E + SEQ * TOP_K // SLOTS - 1
TABLE = MAX_PASSES + 1
UNITS = 12
GATE_UNITS = 4
UNIT = 2 * F
AHEAD = 24
NOT_ROUTED = -16384.0

C_ID = 0
C_TRI = C_ID + P
C_TRI_IN = C_TRI + P
C_ONE = C_TRI_IN + E
C_IOTA = C_ONE + P
C_COSA = C_IOTA + 2 * SLOTS
C_SINA = C_COSA + TC * HD
C_COSB = C_SINA + TC * HD
C_SINB = C_COSB + TC * HD
C_LOGM = C_SINB + TC * HD
C_END = C_LOGM + TC * SEQ

PROJ = (
    ("qa", 0, 512, 0),
    ("kva", 512, 256, 2),
    ("vb", 1792, 512, 3),
    ("qb", 768, 512, 5),
    ("kb", 1280, 512, 7),
)
PROJ_UNITS = 9
PROJ_BANK = (4, 5, 6, 7, 0, 1, 1, 2, 1, 2)
S_BANK = (3, 4)
PT_BANK = (5, 6)
O_BANK = (7, 0)
OPA_BANK = (1, 2, 1, 2)
OPB_BANK = (5, 6, 7, 0)
PAIRS = tuple((j, j + GROUP_A) for j in range(GROUP_A)) + \
    tuple((HEADS_A + 2 * j, HEADS_A + 2 * j + 1) for j in range(HEADS_B // 2))
A_PAIRS = HEADS_A // 2
SP_BANK = (7, 6, 3, 4)

R_MAX = 3
R_SEL = 14
R_NPASS = 20
R_WT = 22
R_PICK = 28
R_PSUM = 31


def constants():
    c = np.zeros((P, C_END), np.float32)
    c[:, C_ID:C_ID + P] = np.eye(P)
    t = np.arange(P)
    c[:, C_TRI:C_TRI + P] = t[:, None] < t[None, :]
    e = np.arange(E)
    c[:E, C_TRI_IN:C_TRI_IN + E] = e[:, None] <= e[None, :]
    c[:, C_ONE:C_ONE + P] = 1.0
    c[:, C_IOTA:C_IOTA + 2 * SLOTS] = np.arange(2 * SLOTS) % SLOTS
    pos = np.arange(SEQ)

    def angles(at, dim):
        inv = np.float32(THETA) ** (-np.arange(0, dim, 2, dtype=np.float32) / np.float32(dim))
        return at.astype(np.float32)[:, None] * inv[None, :].astype(np.float32)

    row, col, one = angles(pos // GRID_W, HD // 2), angles(pos % GRID_W, HD // 2), angles(pos, HD)
    cos_a = np.concatenate([np.cos(row), np.cos(row), np.cos(col), np.cos(col)], 1)
    sin_a = np.concatenate([-np.sin(row), np.sin(row), -np.sin(col), np.sin(col)], 1)
    cos_b = np.concatenate([np.cos(one), np.cos(one)], 1)
    sin_b = np.concatenate([-np.sin(one), np.sin(one)], 1)
    for at, table in ((C_COSA, cos_a), (C_SINA, sin_a), (C_COSB, cos_b), (C_SINB, sin_b)):
        c[:, at:at + TC * HD] = table.reshape(TC, P, HD).transpose(1, 0, 2).reshape(P, TC * HD)
    delta = pos[None, :] - pos[:, None]
    times = sum(((delta % dil == 0) & (abs(delta) <= window // 2)).astype(np.float32)
                for window, dil in BRANCHES)
    logm = np.where(times > 0, np.log(np.maximum(times, 1.0)), -1e30).astype(np.float32)
    c[:, C_LOGM:C_END] = logm.reshape(TC, P, SEQ).transpose(1, 0, 2).reshape(P, TC * SEQ)
    return c


def encoder_kernel(nc, x, attn_norm, w_in, q_norm, k_norm, out_norm_a, out_norm_b, w_out,
                   ffn_norm, w_router, b_router, w_gate, b_gate, w_up, b_up, w_down, b_down,
                   final_norm, consts, out):
    with ExitStack() as ctx:
        def sb(name, shape, dt=F32):
            return ctx.enter_context(nc.sbuf_tensor(name, shape, dt))

        def sem(name):
            return ctx.enter_context(nc.semaphore(name))

        ring = sb("ring", [P, (UNITS + GATE_UNITS) * UNIT])
        wout = sb("wout", [P, KC, D])
        acc = sb("acc", [P, TC, D])
        xs = sb("xs", [P, TC, D])

        def in_unit(u, at, *dims):
            n = int(np.prod(dims))
            v = ring[:, (GATE_UNITS + u) * UNIT + at:(GATE_UNITS + u) * UNIT + at + n]
            if len(dims) == 2:
                return v.rearrange("p (a b) -> p a b", b=dims[1])
            return v.rearrange("p (a b c d) -> p a b c d", b=dims[1], c=dims[2], d=dims[3])

        qr = in_unit(0, 0, TC, HEADS * HD)
        kr = in_unit(1, 0, TC, (KV_A + HEADS_B) * HD)
        rot = in_unit(1, TC * (KV_A + HEADS_B) * HD, 3, 2, TC, HD)
        work = in_unit(2, 0, 4, 512)
        hT = in_unit(3, 0, KC, SEQ)
        vv = sb("vv", [P, TC, (KV_A + HEADS_B) * HD])
        qT = sb("qT", [P, HEADS // 2, SEQ])
        kT = sb("kT", [P, (KV_A + HEADS_B) // 2, SEQ])
        part2 = sb("part2", [P, 512])
        masked = hT[:, 4:8, :].rearrange("p (b c) k -> p b c k", b=2)
        cst = sb("cst", [P, C_END])
        vecs = sb("vecs", [3 * KC, P])
        gains = sb("gains", [P, 3 * KC])
        fgain = kT[:, 0:4, :].rearrange("p k s -> p (k s)")
        qkg = sb("qkg", [P, 2, HD])
        wr = sb("wr", [P, KC, E])
        brt = sb("brt", [P, E])
        vv_flat = vv[:, :, :].rearrange("p c n -> p (c n)")
        bd = vv_flat[0:E, 0:D].rearrange("e (j n) -> e j n", j=2)
        bu = cst[0:E, C_COSA:C_COSA + F]
        bg = wout[0:E, KC - 1, :]
        ss = sb("ss", [P, 16])
        ms = sb("ms", [P, 16])
        rsq = sb("rsq", [P, TC])
        nhalf = sb("nhalf", [P, HEADS_A])
        rstd = sb("rstd", [P, 16])
        hss = sb("hss", [P, 4, HEADS_A])
        hms = sb("hms", [P, 4, HEADS_A])
        hrp = sb("hrp", [P, 4, HEADS_A])
        hrs = sb("hrs", [P, 4, HEADS_A])
        mx = sb("mx", [P, HEADS, TC])
        nmx = sb("nmx", [P, HEADS, TC])
        rs = sb("rs", [P, TC, HEADS])
        ri = sb("ri", [P, TC, HEADS])
        m8 = sb("m8", [P, TC, 8])
        room = sb("room", [P, TC])
        more = sb("more", [P, TC])
        nv0 = sb("nv0", [P, TC])
        den = sb("den", [P, TC])
        rden = sb("rden", [P, TC])
        npass = sb("npass", [E, 4])
        cum = sb("cum", [E, 2])
        ohA, oh, ohz = (vv_flat[0:E, D + i * TABLE:D + (i + 1) * TABLE] for i in range(3))
        p64 = sb("p64", [P, TABLE])
        base = sb("base", [P, TABLE])
        slot_p = sb("slot_p", [P, TC, TABLE])
        gate_p = sb("gate_p", [P, TC, TABLE])
        tab = sb("tab", [1, 1 + E], I32)

        q_flat = qT[:, :, :].rearrange("p k s -> p (k s)")
        n_bias = 2 * FC * TABLE
        bias_p = q_flat[:, 0:n_bias].rearrange("p (j m q) -> p j m q", j=2, m=FC)
        rT = q_flat[0:E, n_bias:n_bias + 2 * SEQ].rearrange("e (j s) -> e j s", j=2)

        at = n_bias + 2 * SEQ
        lg, gt, eq, sel, ew, ex, wt, rk, rkc = (
            q_flat[:, at + i * TC * E:at + (i + 1) * TC * E].rearrange("p (c e) -> p c e", c=TC) for i in range(9))
        at += 9 * TC * E
        n_scan = TC * (E + E // 2)
        scan = q_flat[:, at:at + 2 * n_scan].rearrange("p (b c e) -> p b c e", b=2, c=TC)

        wo_flat = wout[:, :, :].rearrange("p k n -> p (k n)")

        def temp(n, size, parts=P):
            return wo_flat[0:parts, n:n + size]

        xT = temp(0, 512).rearrange("p (k s) -> p k s", s=SLOTS)
        g1, g2, sg, gs = (temp(512 * i, 512) for i in (1, 2, 3, 4))
        u1, u2, act_t, yrows = (temp(512 * i, 512) for i in (5, 6, 7, 8))
        grow, urow = temp(512 * 9, 512), temp(512 * 10, 512)
        GT = temp(512 * 11, SEQ)
        S = temp(512 * 12, TC * SLOTS).rearrange("p (c s) -> p c s", s=SLOTS)
        G = temp(512 * 13, TC * 2 * SLOTS).rearrange("p (c s) -> p c s", s=2 * SLOTS)

        prob = work[:, 0:2, :].rearrange("p b (c k) -> p b c k", c=TC)
        probT = work[:, 2:4, :].rearrange("p b (c k) -> p b c k", c=TC)
        o = xs

        banks = [ctx.enter_context(nc.psum_tensor(f"bank{i}", [P, 512], F32)) for i in range(8)]

        ident = cst[:, C_ID:C_ID + P]
        tri = cst[:, C_TRI:C_TRI + P]
        tri_in = cst[0:E, C_TRI_IN:C_TRI_IN + E]
        ones = cst[:, C_ONE:C_ONE + P]
        iota = cst[:, C_IOTA:C_IOTA + SLOTS]
        iota_twice = cst[:, C_IOTA:C_IOTA + 2 * SLOTS]

        def table(at):
            return cst[:, at:at + TC * HD].rearrange("p (c d) -> p c d", c=TC)

        logm = cst[:, C_LOGM:C_END].rearrange("p (c k) -> p c k", c=TC)

        def unit(u, odd=False):
            at = u if u < GATE_UNITS and not odd else GATE_UNITS + u
            return ring[:, at * UNIT:(at + 1) * UNIT]

        x_in = [sem(f"x_in{c}") for c in range(TC)]
        cst_in = sem("cst_in")
        vecs_in = [sem(f"vecs_in{i}") for i in range(4)]
        qkg_in = [sem(f"qkg_in{i}") for i in range(2)]
        proj_in = [sem(f"proj_in{u}") for u in range(PROJ_UNITS)]
        wout_in = [sem(f"wout_in{i}") for i in range(4)]
        wr_in = sem("wr_in")
        brt_in = sem("brt_in")
        bg_in, bu_in, bd_in = sem("bg_in"), sem("bu_in"), sem("bd_in")
        fgain_in = sem("fgain_in")
        unit_in = [sem(f"unit_in{u}") for u in range(UNITS)]
        out_stored = sem("out_stored")
        sq_done = sem("sq_done")
        ms_done = sem("ms_done")
        rstd_done = sem("rstd_done")
        xs_done = sem("xs_done")
        gains_turned, gains_ready = sem("gains_turned"), sem("gains_ready")
        rot_ready = sem("rot_ready")
        x_turned = sem("x_turned")
        hT_ready = sem("hT_ready")
        proj_done = sem("proj_done")
        hsq_done, hss_done = sem("hsq_done"), sem("hss_done")
        hms_done, hrp_done, hrs_done = sem("hms_done"), sem("hrp_done"), sem("hrs_done")
        normed = sem("normed")
        rot_parts = sem("rot_parts")
        rope_ready = sem("rope_ready")
        v_ready = sem("v_ready")
        qk_turned = sem("qk_turned")
        qkT_ready = sem("qkT_ready")
        scores_done = sem("scores_done")
        masked_ready = sem("masked_ready")
        mx_ready, nmx_ready = sem("mx_ready"), sem("nmx_ready")
        prob_ready = sem("prob_ready")
        prob_turned = sem("prob_turned")
        probTa_ready, probTb_ready = sem("probTa_ready"), sem("probTb_ready")
        pv_done = sem("pv_done")
        ri_ready = sem("ri_ready")
        o_ready = sem("o_ready")
        ident_in = sem("ident_in")
        nhalf_ready = sem("nhalf_ready")
        oproj_done = sem("oproj_done")
        x1_ready = sem("x1_ready")
        logits_done = sem("logits_done")
        r_step = sem("r_step")
        exp_ready = sem("exp_ready")
        ranks_done, cum_done, turned_done = sem("ranks_done"), sem("cum_done"), sem("turned_done")
        picks_done, biases_done = sem("picks_done"), sem("biases_done")
        bdown_done = sem("bdown_done")
        biasg_ready, biasu_ready = sem("biasg_ready"), sem("biasu_ready")
        p64_ready = sem("p64_ready")
        tab_ready = sem("tab_ready")
        unit_used = [sem(f"unit_used{u}") for u in range(UNITS)]
        gathered, xT_ready = sem("gathered"), sem("xT_ready")
        S_ready, G_ready = sem("S_ready"), sem("G_ready")
        gate_biased, gate_clamped = sem("gate_biased"), sem("gate_clamped")
        sig_ready, gs_ready = sem("sig_ready"), sem("gs_ready")
        up_biased, up_clamped, act_ready = sem("up_biased"), sem("up_clamped"), sem("act_ready")
        grow_ready, urow_ready = sem("grow_ready"), sem("urow_ready")
        gate_turned, up_turned = sem("gate_turned"), sem("up_turned")
        G_turned, GT_ready = sem("G_turned"), sem("GT_ready")
        yrows_ready = sem("yrows_ready")
        spread = [sem(f"spread{i}") for i in range(4)]
        added = [sem(f"added{i}") for i in range(4)]
        fin_scaled = sem("fin_scaled")
        fin_ready = sem("fin_ready")

        block = ctx.enter_context(nc.Block())

        w_by_unit = [(w, 2 * j) for w in (w_gate, w_up, w_down) for j in range(4)]

        def load_unit(sp, u, e, odd=False):
            w, k = w_by_unit[u]
            src = w[0, e, k * P:(k + 2) * P, :] if isinstance(e, int) else \
                w[0, bass.ds(e, 1), k * P:(k + 2) * P, :].rearrange("e r n -> (e r) n")
            sp.dma_start(unit(u, odd).rearrange("p (k n) -> p k n", k=2),
                         src.rearrange("(k p) n -> p k n", p=P)).then_inc(unit_in[u], 16)

        @block.sync
        def _(sp):
            sp.dma_start(cst[:, 0:P], consts[:, 0:P]).then_inc(ident_in, 16)
            for c in range(TC):
                sp.dma_start(acc[:, c, :], x[0, c * P:(c + 1) * P, :]).then_inc(x_in[c], 16)
            for _, col, width, u0 in PROJ:
                rows = UNIT // width
                for j in range(KC // rows):
                    sp.dma_start(
                        unit(u0 + j).rearrange("p (k n) -> p k n", n=width),
                        w_in[0, j * rows * P:(j + 1) * rows * P, col:col + width]
                        .rearrange("(k p) n -> p k n", p=P)).then_inc(proj_in[u0 + j], 16)
                if u0 == 0:
                    sp.dma_start(cst[:, P:], consts[:, P:]).then_inc(cst_in, 16)
            for i in range(4):
                sp.dma_start(wout[:, 2 * i:2 * i + 2, :],
                             w_out[0, 2 * i * P:2 * (i + 1) * P, :]
                             .rearrange("(k p) n -> p k n", p=P)).then_inc(wout_in[i], 16)
            for u in range(PROJ_UNITS, UNITS):
                load_unit(sp, u, 0)
            for g, (_, _, width, u0) in enumerate(PROJ):
                sp.wait_ge(proj_done, 2 * g + 2)
                for j in range(KC * width // UNIT):
                    load_unit(sp, u0 + j, 0)
            for u, (read, n) in enumerate(((qk_turned, 7), (qk_turned, 7), (pv_done, len(PAIRS)), (logits_done, 1))):
                sp.wait_ge(read, n)
                sp.wait_ge(unit_in[u], 16)
                load_unit(sp, u, 1, odd=True)
            sp.wait_ge(tab_ready, 1)

            def up_and_down(e, upto):
                for u in range(GATE_UNITS, UNITS):
                    sp.wait_ge(unit_used[u], upto)
                    load_unit(sp, u, e)

            def gates(e, odd, upto, landed):
                for u in range(GATE_UNITS):
                    sp.wait_ge(unit_used[u], upto)
                    sp.wait_ge(unit_in[u], landed)
                    load_unit(sp, u, e, odd)

            def passes_upto(e):
                at = slice(e + 1, e + 2) if isinstance(e, int) else bass.ds(e + 1, 1)
                return sp.value_load(tab[0:1, at], min_val=1, max_val=MAX_PASSES)

            with sp.Fori(0, AHEAD // 2) as pair:
                for odd in (False, True):
                    e = pair * 2 + int(odd)
                    upto = passes_upto(e)
                    gates(e + 2, odd, upto, sp.snap(e * 16 + 32))
                    up_and_down(e + 1, upto)
            up_and_down(AHEAD + 1, passes_upto(AHEAD))
            with sp.Fori(0, (E - AHEAD - 3) // 2) as pair:
                for odd in (False, True):
                    e = pair * 2 + (AHEAD + 2 + int(odd))
                    gates(e, odd, passes_upto(e - 2), sp.snap(e * 16))
                    up_and_down(e, passes_upto(e - 1))
            for e in range(E - 2, E):
                gates(e, e % 2 == 1, passes_upto(e - 2), 16 * e)
                up_and_down(e, passes_upto(e - 1))
            for c in range(TC):
                sp.wait_ge(fin_ready, c + 1)
                sp.dma_start(out[0, c * P:(c + 1) * P, :], xs[:, c, :]).then_inc(out_stored, 16)
            sp.wait_ge(out_stored, 16 * TC)

        @block.gpsimd
        def _(pool):
            pool.memset(nhalf[:, :], -0.5).then_inc(nhalf_ready, 1)
            pool.wait_ge(nhalf_ready, 1)

            def norms(n, n_sq, a, width, chunks=TC):
                b = a + chunks
                pool.wait_ge(sq_done, n_sq)
                pool.tensor_scalar(ms[:, a:b], ss[:, a:b], 1.0 / width, EPS, ALU.mult, ALU.add).then_inc(ms_done, 1)
                pool.wait_ge(ms_done, n)
                pool.tensor_tensor(rstd[:, a:b], ms[:, a:b], nhalf[:, 0:chunks], ALU.pow).then_inc(rstd_done, 1)

            norms(1, 2, 0, D)
            pool.wait_ge(rstd_done, 1)
            pool.tensor_tensor(rsq[:, :], rstd[:, 0:2], rstd[:, 0:2], ALU.mult).then_inc(hms_done, 1)
            pool.wait_ge(hms_done, 1)
            for i, heads in enumerate((HEADS_A, HEADS_A, KV_A, KV_A)):
                c = i % 2
                pool.wait_ge(hss_done, i + 1)
                pool.tensor_scalar(hms[:, i, 0:heads], hss[:, i, 0:heads], rsq[:, c:c + 1], None, ALU.mult)\
                    .then_inc(hms_done, 1)
                pool.wait_ge(hms_done, 2 * i + 2)
                pool.tensor_scalar(hms[:, i, 0:heads], hms[:, i, 0:heads], 1.0 / HD, EPS, ALU.mult, ALU.add)\
                    .then_inc(hms_done, 1)
                pool.wait_ge(hms_done, 2 * i + 3)
                pool.tensor_tensor(hrp[:, i, 0:heads], hms[:, i, 0:heads], nhalf[:, 0:heads], ALU.pow)\
                    .then_inc(hrp_done, 1)
                pool.wait_ge(hrp_done, i + 1)
                pool.tensor_scalar(hrs[:, i, 0:heads], hrp[:, i, 0:heads], rstd[:, c:c + 1], None, ALU.mult)\
                    .then_inc(hrs_done, 1)
            norms(2, 4, 2, 512)
            pool.wait_ge(cst_in, 16)
            pool.tensor_scalar(p64[:, :], iota[:, 0:TABLE], float(SLOTS), 0.0, ALU.mult, ALU.add)\
                .then_inc(p64_ready, 1)
            norms(3, 6, 4, 512)
            norms(4, 8, 6, D)
            norms(5, 9, 8, D, 1)
            norms(6, 10, 9, D, 1)

        @block.scalar
        def _(act):
            for i, (v, a, n) in enumerate(((attn_norm, 0, KC), (ffn_norm, KC, KC),
                                           (out_norm_a, 2 * KC, KC // 2),
                                           (out_norm_b, 2 * KC + KC // 2, KC // 2))):
                act.dma_start(vecs[a:a + n, :], v[0, :].rearrange("(k p) -> k p", p=P)).then_inc(vecs_in[i], 16)
            for i, v in enumerate((q_norm, k_norm)):
                act.dma_start(qkg[:, i, :], v.broadcast_to([P, HD])).then_inc(qkg_in[i], 16)

            def sum_squares(src, junk, col):
                act.activation(junk, src, ACT.Square, accum_out=ss[:, col:col + 1]).then_inc(sq_done, 1)

            for c in range(TC):
                act.wait_ge(x_in[c], 16)
                sum_squares(acc[:, c, :], xs[:, c, :], c)
            act.dma_start(wr[:, :, :], w_router[0].rearrange("(k p) e -> p k e", p=P)).then_inc(wr_in, 16)
            act.dma_start(brt[:, :], b_router.broadcast_to([P, E])).then_inc(brt_in, 16)

            for i, heads in enumerate((HEADS_A, HEADS_A, KV_A, KV_A)):
                act.wait_ge(proj_done, i + 1)
                w = heads * HD
                if i >= 1:
                    act.wait_ge(hss_done, i)
                act.activation(work[:, 3, 0:w], banks[PROJ_BANK[i]][:, 0:w], ACT.Square).then_inc(hsq_done, 1)
                if i == 2:
                    act.wait_ge(rstd_done, 1)
                if i >= 2:
                    act.activation(vv[:, i % 2, 0:KV_A * HD], banks[PROJ_BANK[i]][:, w:2 * w], ACT.Copy,
                                   scale=rstd[:, i % 2:i % 2 + 1]).then_inc(v_ready, 1)
            for i in (4, 5):
                act.wait_ge(proj_done, i + 1)
                act.activation(vv[:, i % 2, KV_A * HD:], banks[PROJ_BANK[i]][:, :], ACT.Copy,
                               scale=rstd[:, i % 2:i % 2 + 1]).then_inc(v_ready, 1)

            def qk_copy(n):
                dst, w, bank = ((qT[:, 0:2, :], 512, 2), (qT[:, 2:4, :], 512, 3), (kT[:, 0:1, :], 256, 4),
                                (qT[:, 4:6, :], 512, 2), (qT[:, 6:8, :], 512, 3),
                                (kT[:, 1:3, :], 512, 1), (kT[:, 3:5, :], 512, 2))[n]
                act.wait_ge(qk_turned, n + 1)
                act.activation(dst.rearrange("p k s -> p (k s)"), banks[bank][:, 0:w], ACT.Copy).then_inc(qkT_ready, 1)

            for n in range(3):
                qk_copy(n)

            def exps(i, j):
                h = PAIRS[i][j]
                act.wait_ge(nmx_ready, 2 * i + j + 1)
                if i >= 1:
                    act.wait_ge(prob_turned, 2 * i - 1 + j)
                for c in range(TC):
                    src = banks[S_BANK[j]][:, c * SEQ:(c + 1) * SEQ] if i < A_PAIRS else masked[:, j, c, :]
                    last = act.activation(prob[:, j, c, :], src, ACT.Exp, bias=nmx[:, h, c:c + 1],
                                          scale=SCALE if i < A_PAIRS else 1.0, accum_out=rs[:, c, h:h + 1])
                last.then_inc(prob_ready, 1)

            def squares_of_outputs(half):
                act.wait_ge(o_ready, 4 * half + 4)
                for c in range(TC):
                    if half or c:
                        act.wait_ge(sq_done, 2 + 2 * half + c)
                    sum_squares(o[:, c, half * 512:(half + 1) * 512], part2[:, :], 2 + 2 * half + c)

            for i in range(len(PAIRS)):
                if i == A_PAIRS:
                    qk_copy(5)
                    qk_copy(6)
                    squares_of_outputs(0)
                exps(i, 0)
                exps(i, 1)
                act.wait_ge(prob_turned, 2 * i + 2)
                if i >= 1:
                    act.wait_ge(pv_done, i)
                act.activation(probT[:, 1, :, :].rearrange("p c k -> p (c k)"), banks[PT_BANK[1]][:, :],
                               ACT.Copy).then_inc(probTb_ready, 1)
                if i == A_PAIRS - 2:
                    qk_copy(3)
                    qk_copy(4)

            act.dma_start(fgain, final_norm.rearrange("(a d) -> a d", a=1).broadcast_to([P, D])).then_inc(fgain_in, 16)
            squares_of_outputs(1)
            act.dma_start(bu, b_up[0]).then_inc(bu_in, 16)
            act.dma_start(bd, b_down[0].rearrange("e (j n) -> e j n", j=2)).then_inc(bd_in, 16)
            act.wait_ge(oproj_done, 8)
            act.dma_start(bg, b_gate[0]).then_inc(bg_in, 16)
            for c in range(TC):
                act.wait_ge(x1_ready, 6 + 2 * c)
                sum_squares(acc[:, c, :], qT[:, 4 * c:4 * c + 4, :].rearrange("p k s -> p (k s)"), 6 + c)

            act.wait_ge(r_step, R_MAX)
            for c in range(TC):
                last = act.activation(ex[:, c, :], lg[:, c, :], ACT.Exp, bias=nv0[:, c:c + 1])
            last.then_inc(exp_ready, 1)
            act.wait_ge(tab_ready, 1)
            passes = act.value_load(tab[0:1, E:1 + E], min_val=1, max_val=MAX_PASSES)

            def one_pass(p, first):
                act.wait_ge(unit_used[3], p + 1)
                if not first:
                    act.wait_ge(gate_turned, p)
                act.activation(grow, banks[1][:, :], ACT.Copy).then_inc(grow_ready, 1)
                act.wait_ge(gate_clamped, p + 1)
                act.activation(sg, g2, ACT.Sigmoid, scale=ALPHA).then_inc(sig_ready, 1)
                if first:
                    act.wait_ge(biases_done, 2)
                    act.activation(bias_p[:, 1, :, :].rearrange("p m q -> p (m q)"), banks[7][:, 0:FC * TABLE],
                                   ACT.Copy).then_inc(biasu_ready, 1)
                act.wait_ge(unit_used[7], p + 1)
                act.activation(urow, banks[2][:, :], ACT.Copy).then_inc(urow_ready, 1)
                act.wait_ge(G_turned, p + 1)
                act.activation(GT, banks[6][:, 0:SEQ], ACT.Copy).then_inc(GT_ready, 1)
                act.wait_ge(unit_used[UNITS - 1], p + 1)
                act.activation(yrows, banks[3][:, :], ACT.Copy).then_inc(yrows_ready, 1)

            one_pass(0, True)
            with act.Fori(1, passes) as p:
                one_pass(p, False)

            for c in range(TC):
                act.wait_ge(added[2 * c], passes + 1)
                act.wait_ge(added[2 * c + 1], passes + 1)
                sum_squares(acc[:, c, :], wo_flat[:, c * D:(c + 1) * D], 8 + c)

        @block.tensor
        def _(pe):
            pe.wait_ge(ident_in, 16)
            for i in range(4):
                pe.wait_ge(vecs_in[i], 16)
            pe.transpose(banks[7][:, 0:3 * KC], vecs[:, :], ident[0:3 * KC, 0:3 * KC]).then_inc(gains_turned, 1)

            def turn_rows(src, bank_of, chunks=range(KC)):
                for n, k in enumerate(chunks):
                    for c in range(TC):
                        last = pe.transpose(banks[bank_of[n // 2]][:, k % 2 * SEQ + c * P:k % 2 * SEQ + (c + 1) * P],
                                            src[:, c, k * P:(k + 1) * P], ident)
                    if k % 2:
                        last.then_inc(x_turned, 1)

            for c in range(TC):
                pe.wait_ge(x_in[c], 16)
            turn_rows(acc, (0, 1, 2, 3))

            def project(i):
                _, _, width, u0 = PROJ[i // 2]
                c, rows = i % 2, UNIT // width
                if i == 3:
                    pe.wait_ge(gains_ready, 1)
                if i == 6:
                    pe.wait_ge(v_ready, 4)
                if i == 8:
                    pe.wait_ge(rope_ready, 5)
                if i == 9:
                    pe.wait_ge(rope_ready, 6)
                    pe.wait_ge(qkT_ready, 4)
                for k in range(KC):
                    if c == 0:
                        pe.wait_ge(proj_in[u0 + k // rows], 16)
                    if i == 0:
                        pe.wait_ge(hT_ready, k // 2 + 1)
                    last = pe.matmul(banks[PROJ_BANK[i]][:, 0:width], hT[:, k, c * P:(c + 1) * P],
                                     unit(u0 + k // rows)[:, (k % rows) * width:(k % rows + 1) * width],
                                     start=(k == 0), stop=(k == KC - 1))
                last.then_inc(proj_done, 1)

            def turn_pairs(src, pairs, bank):
                for n, pair in enumerate(pairs):
                    for c in range(TC):
                        last = pe.transpose(banks[bank][:, n * SEQ + c * P:n * SEQ + (c + 1) * P],
                                            src[:, c, pair * P:(pair + 1) * P], ident)
                last.then_inc(qk_turned, 1)

            for i in range(6):
                project(i)
            pe.wait_ge(rope_ready, 4)
            turn_pairs(qr, (0, 1), 2)
            turn_pairs(qr, (2, 3), 3)
            turn_pairs(kr, (0,), 4)

            def scores(i):
                kpair = 0 if i < A_PAIRS else 1 + i - A_PAIRS
                pe.wait_ge(qkT_ready, 3 if i < A_PAIRS - 1 else 5 if i < A_PAIRS else 7)
                if i >= 1:
                    pe.wait_ge(prob_ready, 2 * i)
                for c in range(TC):
                    for j in range(2):
                        half = slice(j * HD, (j + 1) * HD)
                        last = pe.matmul(banks[S_BANK[j]][:, c * SEQ:(c + 1) * SEQ], qT[half, i, c * P:(c + 1) * P],
                                         kT[half, kpair, :], start=True, stop=True)
                last.then_inc(scores_done, 1)

            def turn_probs(i):
                for j in range(2):
                    pe.wait_ge(prob_ready, 2 * i + j + 1)
                    if i >= 1:
                        pe.wait_ge(probTa_ready if j == 0 else probTb_ready, i)
                    for kc in range(TC):
                        for c in range(TC):
                            last = pe.transpose(banks[PT_BANK[j]][:, kc * SEQ + c * P:kc * SEQ + (c + 1) * P],
                                                prob[:, j, c, kc * P:(kc + 1) * P], ident)
                    last.then_inc(prob_turned, 1)

            def weigh_values(i):
                if i >= 2:
                    pe.wait_ge(o_ready, i - 1)
                for j, h in enumerate(PAIRS[i]):
                    pe.wait_ge(probTa_ready if j == 0 else probTb_ready, i + 1)
                    vh = h // GROUP_A if h < HEADS_A else KV_A + h - HEADS_A
                    for c in range(TC):
                        for kc in range(TC):
                            last = pe.matmul(banks[O_BANK[i % 2]][:, c * P + j * HD:c * P + (j + 1) * HD],
                                             probT[:, j, kc, c * P:(c + 1) * P], vv[:, kc, vh * HD:(vh + 1) * HD],
                                             start=(kc == 0), stop=(kc == TC - 1))
                last.then_inc(pv_done, 1)

            def project_out(half, i):
                c, n = i // 2, i % 2
                if half == 0 and i >= 2:
                    pe.wait_ge(x1_ready, i - 1)
                for k in range(4 * half, 4 * half + 4):
                    pe.wait_ge(hT_ready, 4 + k // 2 + 1)
                    if i == 0:
                        pe.wait_ge(wout_in[k // 2], 16)
                    last = pe.matmul(banks[(OPA_BANK, OPB_BANK)[half][i]][:, :], hT[:, k, c * P:(c + 1) * P],
                                     wout[:, k, n * 512:(n + 1) * 512], start=(k % 4 == 0), stop=(k % 4 == 3))
                last.then_inc(oproj_done, 1)

            for i in range(A_PAIRS):
                scores(i)
                if i >= 1:
                    weigh_values(i - 1)
                project(6 + i)
                turn_probs(i)
                if i == A_PAIRS - 2:
                    pe.wait_ge(rope_ready, 6)
                    turn_pairs(qr, (4, 5), 2)
                    turn_pairs(qr, (6, 7), 3)
            weigh_values(A_PAIRS - 1)
            pe.wait_ge(rope_ready, 8)
            turn_pairs(kr, (1, 2), 1)
            turn_pairs(kr, (3, 4), 2)
            pe.wait_ge(o_ready, A_PAIRS)
            pe.wait_ge(qkT_ready, 7)
            turn_rows(o, (1, 2), range(0, 4))
            for i in range(A_PAIRS, len(PAIRS)):
                scores(i)
                if i > A_PAIRS:
                    weigh_values(i - 1)
                project_out(0, i - A_PAIRS)
                turn_probs(i)
            weigh_values(len(PAIRS) - 1)
            pe.wait_ge(o_ready, len(PAIRS))
            turn_rows(o, (3, 4), range(4, 8))
            for i in range(4):
                project_out(1, i)

            pe.wait_ge(x1_ready, 8)
            turn_rows(acc, (1, 2, 3, 4))
            pe.wait_ge(wr_in, 16)
            for c in range(TC):
                for k in range(KC):
                    pe.wait_ge(hT_ready, 8 + k // 2 + 1)
                    last = pe.matmul(banks[5][:, c * E:(c + 1) * E], hT[:, k, c * P:(c + 1) * P], wr[:, k, :],
                                     start=(k == 0), stop=(k == KC - 1))
            last.then_inc(logits_done, 1)
            pe.wait_ge(cst_in, 16)
            pe.wait_ge(r_step, R_SEL)
            pe.matmul(banks[6][:, 0:E], tri, sel[:, 0, :], start=True, stop=True)
            pe.matmul(banks[6][:, E:2 * E], tri, sel[:, 1, :], start=True, stop=False)
            pe.matmul(banks[6][:, E:2 * E], ones, sel[:, 0, :], start=False, stop=True)
            pe.matmul(banks[6][0:E, 2 * E:2 * E + 1], sel[:, 0, :], ones[:, 0:1], start=True, stop=False)
            pe.matmul(banks[6][0:E, 2 * E:2 * E + 1], sel[:, 1, :], ones[:, 0:1], start=False, stop=True)\
              .then_inc(ranks_done, 1)
            pe.wait_ge(r_step, R_NPASS)
            pe.matmul(banks[0][0:E, 0:1], tri_in, npass[:, 3:4], start=True, stop=True).then_inc(cum_done, 1)
            pe.wait_ge(r_step, R_WT)
            for c in range(TC):
                pe.transpose(banks[1][0:E, c * P:(c + 1) * P], rkc[:, c, :], ident)
                last = pe.transpose(banks[1][0:E, SEQ + c * P:SEQ + (c + 1) * P], wt[:, c, :], ident)
            last.then_inc(turned_done, 1)
            pe.wait_ge(r_step, R_PICK)
            pe.matmul(banks[2][0:1, 0:1], ones[0:1, 0:1], ones[0:1, 0:1], start=True, stop=True)
            pe.matmul(banks[2][0:1, 1:1 + E], cum[:, 0:1], ident[0:E, 0:E], start=True, stop=True)
            pe.matmul(banks[2][:, 128:128 + TABLE], ones[0:E, :], ohz[:, :], start=True, stop=True)
            for c in range(TC):
                for j in range(2):
                    at = 192 + (2 * j + c) * TABLE
                    last = pe.matmul(banks[2][:, at:at + TABLE], rT[:, j, c * P:(c + 1) * P], oh[:, :],
                                     start=True, stop=True)
            last.then_inc(picks_done, 1)
            pe.wait_ge(tab_ready, 1)

            def passes_upto(e):
                return pe.value_load(tab[0:1, bass.ds(e + 1, 1)], min_val=1, max_val=MAX_PASSES)

            pe.wait_ge(xs_done, TC)

            def gather(n_ready, part):
                pe.wait_ge(S_ready, n_ready)
                for k in range(part * KC // 2, (part + 1) * KC // 2):
                    for c in range(TC):
                        last = pe.matmul(banks[0][:, k * SLOTS:(k + 1) * SLOTS], xs[:, c, k * P:(k + 1) * P],
                                         S[:, c, :], start=(c == 0), stop=(c == TC - 1))
                if part:
                    last.then_inc(gathered, 1)

            def product(bank, src, units, landed, odd=False):
                for u in units:
                    pe.wait_ge(unit_in[u], landed)
                    for kk in range(2):
                        k = 2 * (u % 4) + kk
                        for half in range(2):
                            at = kk * F + half * 512
                            last = pe.matmul(banks[bank][half * SLOTS:(half + 1) * SLOTS, :], src(k),
                                             unit(u, odd)[:, at:at + 512], start=(k == 0), stop=(k == KC - 1))
                    last.then_inc(unit_used[u], 1)

            def turn(bank, src, done):
                for m in range(FC // 2):
                    last = pe.transpose(banks[bank][:, m * P:(m + 1) * P], src[:, m * P:(m + 1) * P], ident)
                last.then_inc(done, 1)

            def turn_slots(p, first):
                if not first:
                    pe.wait_ge(added[1], p + 1)
                pe.wait_ge(G_ready, p + 1)
                for c in range(TC):
                    last = pe.transpose(banks[6][:, c * P:(c + 1) * P], G[:, c, :], ident)
                last.then_inc(G_turned, 1)

            def spread_results(p, bank4_read):
                pe.wait_ge(GT_ready, p)
                pe.wait_ge(yrows_ready, p)
                pe.wait_ge(added[0], p)
                for i in range(4):
                    c, n = i // 2, i % 2
                    if i == 3:
                        pe.wait_ge(gate_biased, bank4_read)
                    half = slice(n * SLOTS, (n + 1) * SLOTS)
                    pe.matmul(banks[SP_BANK[i]][:, :], GT[half, c * P:(c + 1) * P], yrows[half, :],
                              start=True, stop=True).then_inc(spread[i], 1)

            def biases(j, b, landed):
                pe.wait_ge(landed, 16)
                for m in range(FC):
                    last = pe.matmul(banks[3 if j == 0 else 7][:, m * TABLE:(m + 1) * TABLE],
                                     b[:, m * P:(m + 1) * P], oh[:, :], start=True, stop=True)
                last.then_inc(biases_done, 1)

            def down_biases():
                pe.wait_ge(bd_in, 16)
                pe.wait_ge(biasu_ready, 1)
                pe.wait_ge(GT_ready, 1)
                pe.wait_ge(yrows_ready, 1)
                pe.wait_ge(gate_biased, 1)
                for c in range(TC):
                    for n in range(2):
                        pe.matmul(banks[SP_BANK[2 * c + n]][:, :], rT[:, 1, c * P:(c + 1) * P], bd[:, n, :],
                                  start=True, stop=True).then_inc(bdown_done, 1)

            def one_pass(p, first, landed, odd):
                pe.wait_ge(xT_ready, p + 1)
                if not first:
                    pe.wait_ge(grow_ready, p)
                product(1, lambda k: xT[:, k, :], range(0, 4), landed, odd)
                if first:
                    biases(0, bg, bg_in)
                else:
                    pe.wait_ge(urow_ready, p)
                product(2, lambda k: xT[:, k, :], range(4, 6), landed)
                pe.wait_ge(grow_ready, p + 1)
                if not first:
                    pe.wait_ge(added[3], p)
                turn(4, grow, gate_turned)
                if first:
                    biases(1, bu, bu_in)
                else:
                    spread_results(p, p + 1)
                product(2, lambda k: xT[:, k, :], range(6, 8), landed)
                gather(p + 2, 0)
                if not first:
                    pe.wait_ge(up_biased, p)
                pe.wait_ge(urow_ready, p + 1)
                turn(5, urow, up_turned)
                gather(p + 2, 1)
                turn_slots(p, first)
                pe.wait_ge(act_ready, p + 1)
                if first:
                    pe.wait_ge(biasg_ready, 1)
                else:
                    pe.wait_ge(added[2], p + 1)
                product(3, lambda k: act_t[:, act_at(k):act_at(k) + SLOTS], range(8, 12), landed)
                if first:
                    down_biases()

            def act_at(k):
                return (k % 4) * 2 * SLOTS + (k // 4) * SLOTS

            gather(1, 0)
            gather(1, 1)
            one_pass(0, True, 16, False)
            with pe.Fori(0, E // 2) as pair:
                for odd in (False, True):
                    e = pair * 2 + int(odd)
                    landed = pe.snap(e * 16 + 16)
                    start, end = passes_upto(e - 1), passes_upto(e)
                    if odd:
                        with pe.Fori(start, end) as p:
                            one_pass(p, False, landed, odd)
                    else:
                        with pe.If(end > start):
                            with pe.Fori(start, end) as p:
                                one_pass(p, False, landed, odd)
            passes = passes_upto(E - 1)
            spread_results(passes, passes)

        @block.vector
        def _(dve):
            dve.wait_ge(gains_turned, 1)
            dve.tensor_copy(gains[:, :], banks[7][:, 0:3 * KC]).then_inc(gains_ready, 1)
            dve.wait_ge(gains_ready, 1)

            def scaled_rows(n, bank_of, col, chunks=range(0, KC, 2)):
                for j, k in enumerate(chunks):
                    dve.wait_ge(x_turned, n + j + 1)
                    g = gains[:, col + k:col + k + 2].unsqueeze(2).broadcast_to([P, 2, SEQ])
                    dve.tensor_tensor(hT[:, k:k + 2, :],
                                      banks[bank_of[j]][:, :].rearrange("p (k s) -> p k s", k=2), g, ALU.mult)\
                       .then_inc(hT_ready, 1)

            scaled_rows(0, (0, 1, 2, 3), 0)

            dve.wait_ge(cst_in, 16)
            for i in range(2):
                dve.wait_ge(qkg_in[i], 16)
                for c in range(TC):
                    dve.tensor_tensor(rot[:, i, 0, c, :], table(C_COSA)[:, c, :], qkg[:, i, :], ALU.mult)
                    for a, b in ((0, 16), (16, 0), (32, 48), (48, 32)):
                        last = dve.tensor_tensor(rot[:, i, 1, c, a:a + 16], table(C_SINA)[:, c, a:a + 16],
                                                 qkg[:, i, b:b + 16], ALU.mult)
            dve.wait_ge(rstd_done, 1)
            for c in range(TC):
                for j, at in enumerate((C_COSB, C_SINB)):
                    last = dve.tensor_scalar(rot[:, 2, j, c, :], table(at)[:, c, :], rstd[:, c:c + 1], None, ALU.mult)
            last.then_inc(rot_ready, 1)
            dve.wait_ge(rot_ready, 1)

            def bc(t, heads):
                return t.unsqueeze(1).broadcast_to([P, heads, t.shape[-1]])

            n_rope = 0

            def rotate(src, dst, view, heads, half, cos, sin):
                nonlocal n_rope
                n_rope += 1
                t2 = part2[:, 0:heads * HD]
                if n_rope > 1:
                    dve.wait_ge(rope_ready, n_rope - 1)
                dve.tensor_tensor(dst, view(src), view_bc(view, cos, heads), ALU.mult)
                for at in range(0, HD, half):
                    other = at + half if at // half % 2 == 0 else at - half
                    last = dve.tensor_tensor(
                        t2.rearrange("p (h d) -> p h d", d=HD)[:, :, at:at + half],
                        src.rearrange("p (h d) -> p h d", d=HD)[:, :, other:other + half],
                        bc(sin[:, at:at + half], heads), ALU.mult)
                last.then_inc(rot_parts, 1)
                dve.wait_ge(rot_parts, n_rope)
                dve.tensor_tensor(dst, dst, view(t2), ALU.add).then_inc(rope_ready, 1)

            def view_bc(view, t, heads):
                if view is by_head:
                    return bc(t, heads)
                return t.unsqueeze(1).unsqueeze(1).broadcast_to([P, 2, heads // 2, HD])

            def by_head(t):
                return t.rearrange("p (h d) -> p h d", d=HD)

            def by_pair(t):
                return t.rearrange("p (two j d) -> p two j d", two=2, d=HD)

            for i, heads in enumerate((HEADS_A, HEADS_A, KV_A, KV_A)):
                c, is_k = i % 2, i // 2
                w = heads * HD
                dve.wait_ge(hsq_done, i + 1)
                dve.tensor_reduce(hss[:, i, 0:heads], by_head(work[:, 3, 0:w]), AX.X, ALU.add).then_inc(hss_done, 1)
                dve.wait_ge(hss_done, i + 1)
                dve.wait_ge(hrs_done, i + 1)
                if is_k:
                    dve.wait_ge(v_ready, c + 1)
                t0 = work[:, 2, 0:w]
                dve.tensor_tensor(by_head(t0), by_head(banks[PROJ_BANK[i]][:, 0:w]),
                                  hrs[:, i, 0:heads].unsqueeze(2).broadcast_to([P, heads, HD]), ALU.mult)\
                   .then_inc(normed, 1)
                dve.wait_ge(normed, i + 1)
                if is_k:
                    rotate(t0, by_head(kr[:, c, 0:w]), by_head, heads, 16, rot[:, 1, 0, c, :], rot[:, 1, 1, c, :])
                else:
                    dst = qr[:, c, 0:w].rearrange("p (j two d) -> p two j d", two=2, d=HD)
                    rotate(t0, dst, by_pair, heads, 16, rot[:, 0, 0, c, :], rot[:, 0, 1, c, :])

            def rotate_b(i):
                c = i % 2
                dve.wait_ge(proj_done, i + 1)
                dst = qr[:, c, HEADS_A * HD:] if i < 8 else kr[:, c, KV_A * HD:]
                rotate(banks[PROJ_BANK[i]][:, :], by_head(dst), by_head, HEADS_B, 32, rot[:, 2, 0, c, :], rot[:, 2, 1, c, :])

            def row_max(i, j):
                h, n = PAIRS[i][j], 2 * i + j
                dve.wait_ge(scores_done, i + 1)
                src = banks[S_BANK[j]][:, :].rearrange("p (c k) -> p c k", c=TC)
                if i < A_PAIRS:
                    dve.tensor_reduce(mx[:, h, :], src, AX.X, ALU.max).then_inc(mx_ready, 1)
                    dve.wait_ge(mx_ready, n + 1)
                    dve.tensor_scalar(nmx[:, h, :], mx[:, h, :], -SCALE, None, ALU.mult).then_inc(nmx_ready, 1)
                else:
                    if i > A_PAIRS:
                        dve.wait_ge(prob_ready, n - 1)
                    dve.scalar_tensor_tensor(out=masked[:, j, :, :], in0=src, scalar=SCALE, in1=logm,
                                             op0=ALU.mult, op1=ALU.add).then_inc(masked_ready, 1)
                    dve.wait_ge(masked_ready, n - 2 * A_PAIRS + 1)
                    dve.tensor_reduce(nmx[:, h, :], masked[:, j, :, :], AX.X, ALU.max, negate=True)\
                       .then_inc(nmx_ready, 1)

            def outputs_of(i):
                step = PAIRS[i][1] - PAIRS[i][0]
                h0 = PAIRS[i][0]
                heads = slice(h0, h0 + step + 1, step)
                dve.wait_ge(prob_ready, 2 * i + 2)
                dve.reciprocal(ri[:, :, heads], rs[:, :, heads]).then_inc(ri_ready, 1)
                dve.wait_ge(ri_ready, i + 1)
                dve.wait_ge(pv_done, i + 1)
                for c in range(TC):
                    last = dve.tensor_tensor(by_head(o[:, c, :])[:, heads, :],
                                             by_head(banks[O_BANK[i % 2]][:, c * P:(c + 1) * P]),
                                             ri[:, c, heads].unsqueeze(2).broadcast_to([P, 2, HD]), ALU.mult)
                last.then_inc(o_ready, 1)

            def onto_stream(half, i):
                c, n = i // 2, i % 2
                part = acc[:, c, n * 512:(n + 1) * 512]
                dve.wait_ge(rstd_done, 2 + half)
                dve.wait_ge(oproj_done, 4 * half + i + 1)
                if half:
                    dve.wait_ge(x1_ready, i + 1)
                dve.scalar_tensor_tensor(out=part, in0=banks[(OPA_BANK, OPB_BANK)[half][i]][:, :],
                                         scalar=rstd[:, 2 + 2 * half + c:3 + 2 * half + c], in1=part,
                                         op0=ALU.mult, op1=ALU.add).then_inc(x1_ready, 1)

            for i in range(len(PAIRS)):
                if i == A_PAIRS:
                    outputs_of(i - 1)
                    scaled_rows(4, (1, 2), 2 * KC, (0, 2))
                row_max(i, 0)
                row_max(i, 1)
                if i >= 1 and i != A_PAIRS:
                    outputs_of(i - 1)
                dve.wait_ge(prob_turned, 2 * i + 1)
                if i >= 1:
                    dve.wait_ge(pv_done, i)
                dve.tensor_copy(probT[:, 0, :, :].rearrange("p c k -> p (c k)"), banks[PT_BANK[0]][:, :])\
                   .then_inc(probTa_ready, 1)
                if i < A_PAIRS:
                    rotate_b(6 + i)
                else:
                    onto_stream(0, i - A_PAIRS)
            outputs_of(len(PAIRS) - 1)
            scaled_rows(6, (3, 4), 2 * KC, (4, 6))
            for i in range(4):
                onto_stream(1, i)
            scaled_rows(8, (1, 2, 3, 4), KC)

            n_step = 0

            def step(ins):
                nonlocal n_step
                n_step += 1
                ins.then_inc(r_step, 1)
                dve.wait_ge(r_step, n_step)

            dve.wait_ge(rstd_done, 4)
            for b in range(2):
                dve.memset(scan[:, b, :, 0:E // 2], 0.0)
            dve.wait_ge(logits_done, 1)
            dve.wait_ge(brt_in, 16)
            for c in range(TC):
                last = dve.scalar_tensor_tensor(out=lg[:, c, :], in0=banks[5][:, c * E:(c + 1) * E],
                                                scalar=rstd[:, 6 + c:7 + c], in1=brt[:, :], op0=ALU.mult, op1=ALU.add)
            step(last)
            for c in range(TC):
                last = dve.max(m8[:, c, :], lg[:, c, :])
            step(last)
            step(dve.tensor_scalar(nv0[:, :], m8[:, :, 0], -1.0, None, ALU.mult))
            assert n_step == R_MAX
            kth = m8[:, :, TOP_K - 1:TOP_K].broadcast_to([P, TC, E])
            pad = E // 2
            dve.tensor_tensor(gt[:, :, :], lg[:, :, :], kth, ALU.is_gt)
            dve.tensor_tensor(eq[:, :, :], lg[:, :, :], kth, ALU.is_equal)
            step(dve.tensor_tensor(scan[:, 0, :, pad:], lg[:, :, :], kth, ALU.is_equal))
            step(dve.tensor_reduce(more[:, :], gt[:, :, :], AX.X, ALU.add))
            step(dve.tensor_scalar(room[:, :], more[:, :], -1.0, float(TOP_K), ALU.mult, ALU.add))
            b = 0
            for shift in (1, 2, 4, 8, 16):
                step(dve.tensor_tensor(scan[:, 1 - b, :, pad:], scan[:, b, :, pad:],
                                       scan[:, b, :, pad - shift:pad + E - shift], ALU.add))
                b = 1 - b
            step(dve.tensor_tensor(ew[:, :, :], scan[:, b, :, pad:], room[:, :].unsqueeze(2).broadcast_to([P, TC, E]),
                                   ALU.is_le))
            step(dve.tensor_tensor(ew[:, :, :], ew[:, :, :], eq[:, :, :], ALU.mult))
            step(dve.tensor_tensor(sel[:, :, :], ew[:, :, :], gt[:, :, :], ALU.add))
            assert n_step == R_SEL
            for c in range(TC):
                dve.tensor_scalar(xs[:, c, :], acc[:, c, :], rstd[:, 6 + c:7 + c], None, ALU.mult).then_inc(xs_done, 1)
            dve.wait_ge(exp_ready, 1)
            step(dve.tensor_tensor(ew[:, :, :], ex[:, :, :], sel[:, :, :], ALU.mult))
            step(dve.tensor_reduce(den[:, :], ew[:, :, :], AX.X, ALU.add))
            step(dve.reciprocal(rden[:, :], den[:, :]))
            step(dve.tensor_tensor(wt[:, :, :], ew[:, :, :], rden[:, :].unsqueeze(2).broadcast_to([P, TC, E]), ALU.mult))
            dve.wait_ge(ranks_done, 1)
            count = banks[6][0:E, 2 * E:2 * E + 1]
            dve.tensor_scalar(npass[:, 0:1], count, float(SLOTS), 1.0, ALU.is_gt, ALU.add)
            dve.tensor_scalar(npass[:, 1:2], count, float(2 * SLOTS), None, ALU.is_gt)
            step(dve.tensor_scalar(npass[:, 2:3], count, float(3 * SLOTS), None, ALU.is_gt))
            step(dve.tensor_reduce(npass[:, 3:4], npass[:, 0:3], AX.X, ALU.add))
            assert n_step == R_NPASS
            step(dve.scalar_tensor_tensor(out=rk[:, :, :], in0=banks[6][:, 0:TC * E].rearrange("p (c e) -> p c e", c=TC),
                                          scalar=-NOT_ROUTED, in1=sel[:, :, :], op0=ALU.add, op1=ALU.mult))
            step(dve.tensor_scalar(rkc[:, :, :], rk[:, :, :], NOT_ROUTED, None, ALU.add))
            assert n_step == R_WT
            dve.wait_ge(cum_done, 1)
            step(dve.tensor_copy(cum[:, 0:1], banks[0][0:E, 0:1]))
            step(dve.tensor_tensor(cum[:, 1:2], cum[:, 0:1], npass[:, 3:4], ALU.subtract))
            numbers = iota[0:E, 0:TABLE]
            step(dve.tensor_scalar(ohA[:, :], numbers, cum[:, 0:1], None, ALU.is_ge))
            step(dve.scalar_tensor_tensor(out=oh[:, :], in0=numbers, scalar=cum[:, 1:2], in1=ohA[:, :],
                                          op0=ALU.is_ge, op1=ALU.subtract))
            step(dve.tensor_scalar(ohz[:, :], oh[:, :], cum[:, 1:2], None, ALU.mult))
            dve.wait_ge(turned_done, 1)
            step(dve.tensor_copy(rT[:, :, :].rearrange("e j s -> e (j s)"), banks[1][0:E, :]))
            assert n_step == R_PICK
            dve.wait_ge(picks_done, 1)
            dve.tensor_copy(tab[:, :], banks[2][0:1, 0:1 + E]).then_inc(tab_ready, 1)
            dve.wait_ge(p64_ready, 1)
            step(dve.scalar_tensor_tensor(out=base[:, :], in0=banks[2][:, 128:128 + TABLE], scalar=float(SLOTS),
                                          in1=p64[:, :], op0=ALU.mult, op1=ALU.subtract))
            pick = banks[2][:, 192:192 + 4 * TABLE].rearrange("p (j c q) -> p j c q", j=2, c=TC)
            step(dve.tensor_tensor(slot_p[:, :, :], pick[:, 0], base[:, :].unsqueeze(1).broadcast_to([P, TC, TABLE]),
                                   ALU.add))
            step(dve.tensor_copy(gate_p[:, :, :], pick[:, 1]))
            assert n_step == R_PSUM

            def slots_of(p):
                for c in range(TC):
                    last = dve.tensor_scalar(S[:, c, :], iota, slot_p[:, c, bass.ds(p, 1)], None, ALU.is_equal)
                last.then_inc(S_ready, 1)

            def gated_slots_of(p):
                for c in range(TC):
                    last = dve.tensor_scalar(G[:, c, :], iota_twice, slot_p[:, c, bass.ds(p, 1)],
                                             gate_p[:, c, bass.ds(p, 1)], ALU.is_equal, ALU.mult)
                last.then_inc(G_ready, 1)

            ffn_gain = gains[:, KC:2 * KC].unsqueeze(2).broadcast_to([P, KC, SLOTS])

            def tokens_out(n):
                dve.wait_ge(gathered, n)
                dve.tensor_tensor(xT, banks[0][:, :].rearrange("p (k s) -> p k s", k=KC), ffn_gain, ALU.mult)\
                   .then_inc(xT_ready, 1)

            def with_bias(dst, bank, j, p):
                for half in range(2):
                    b = bias_p[:, j, half * 4:half * 4 + 4, bass.ds(p, 1)].broadcast_to([P, FC // 2, SLOTS])

                    def part(t):
                        return t.rearrange("p (m h s) -> p h m s", m=FC // 2, h=2)[:, half]
                    last = dve.tensor_tensor(part(dst), part(banks[bank][:, :]), b, ALU.add)
                return last

            def add_up(p):
                for i in range(4):
                    c, n = i // 2, i % 2
                    part = acc[:, c, n * 512:(n + 1) * 512]
                    dve.wait_ge(spread[i], p)
                    dve.wait_ge(added[i], p)
                    dve.tensor_tensor(part, banks[SP_BANK[i]][:, :], part, ALU.add).then_inc(added[i], 1)

            slots_of(0)
            tokens_out(1)

            def one_pass(p, first):
                if first:
                    dve.wait_ge(biases_done, 1)
                    dve.tensor_copy(bias_p[:, 0, :, :].rearrange("p m q -> p (m q)"), banks[3][:, 0:FC * TABLE])\
                       .then_inc(biasg_ready, 1)
                    dve.wait_ge(biasg_ready, 1)
                dve.wait_ge(gate_turned, p + 1)
                with_bias(g1, 4, 0, p).then_inc(gate_biased, 1)
                dve.wait_ge(gate_biased, p + 1)
                dve.tensor_scalar(g2, g1, LIMIT, None, ALU.min).then_inc(gate_clamped, 1)
                dve.wait_ge(gathered, p + 1)
                slots_of(p + 1)
                if not first:
                    dve.wait_ge(G_turned, p)
                gated_slots_of(p)
                dve.wait_ge(gate_clamped, p + 1)
                dve.wait_ge(sig_ready, p + 1)
                dve.tensor_tensor(gs, g2, sg, ALU.mult).then_inc(gs_ready, 1)
                if not first:
                    add_up(p)
                if first:
                    dve.wait_ge(biasu_ready, 1)
                dve.wait_ge(up_turned, p + 1)
                with_bias(u1, 5, 1, p).then_inc(up_biased, 1)
                dve.wait_ge(up_biased, p + 1)
                dve.tensor_scalar(u2, u1, -LIMIT, LIMIT, ALU.max, ALU.min).then_inc(up_clamped, 1)
                dve.wait_ge(up_clamped, p + 1)
                dve.wait_ge(gs_ready, p + 1)
                if not first:
                    dve.wait_ge(unit_used[UNITS - 1], p)
                dve.scalar_tensor_tensor(out=act_t, in0=u2, scalar=1.0, in1=gs, op0=ALU.add, op1=ALU.mult)\
                   .then_inc(act_ready, 1)
                tokens_out(p + 2)
                if first:
                    for i in range(4):
                        c, n = i // 2, i % 2
                        part = acc[:, c, n * 512:(n + 1) * 512]
                        dve.wait_ge(bdown_done, i + 1)
                        dve.tensor_tensor(part, banks[SP_BANK[i]][:, :], part, ALU.add).then_inc(added[i], 1)

            dve.wait_ge(tab_ready, 1)
            passes = dve.value_load(tab[0:1, E:1 + E], min_val=1, max_val=MAX_PASSES)
            one_pass(0, True)
            with dve.Fori(1, passes) as p:
                one_pass(p, False)
            add_up(passes)

            dve.wait_ge(fgain_in, 16)
            for c in range(TC):
                dve.wait_ge(rstd_done, 5 + c)
                dve.scalar_tensor_tensor(out=xs[:, c, :], in0=acc[:, c, :], scalar=rstd[:, 8 + c:9 + c],
                                         in1=fgain, op0=ALU.mult, op1=ALU.mult).then_inc(fin_ready, 1)


INS = ("x", "attn_norm", "w_in", "q_norm", "k_norm", "out_norm_a", "out_norm_b", "w_out", "ffn_norm",
       "w_router", "b_router", "w_gate", "b_gate", "w_up", "b_up", "w_down", "b_down", "final_norm")


def kernel(**inputs):
    import concourse.bacc as bacc
    from concourse.bass_utils import run_bass_kernel_spmd

    nc = bacc.Bacc("TRN2", target_bir_lowering=False, num_devices=1)
    arrays, args = {}, []
    for name in INS:
        arrays[name] = np.ascontiguousarray(inputs[name])
    arrays["consts"] = constants()
    for name, a in arrays.items():
        args.append(nc.dram_tensor(name, a.shape, F32, kind="ExternalInput").ap())
    out = nc.dram_tensor("out", arrays["x"].shape, F32, kind="ExternalOutput").ap()
    encoder_kernel(nc, *args, out)
    r = run_bass_kernel_spmd(nc, [arrays], core_ids=[0])
    return r.results[0]["out"]
```

```python
from contextlib import ExitStack

import concourse.bass as bass
import numpy as np
from concourse import mybir

ALU = mybir.AluOpType
ACT = mybir.ActivationFunctionType
AX = mybir.AxisListType
F32 = mybir.dt.float32
I32 = mybir.dt.int32

P = 128
SEQ = 256
D = 1024
TC = SEQ // P
KC = D // P
HD = 64
HEADS_A, KV_A, HEADS_B = 8, 2, 8
HEADS = HEADS_A + HEADS_B
GROUP_A = HEADS_A // KV_A
BRANCHES = ((128, 1), (512, 4), (2048, 16))
GRID_W = 64
THETA = 10000.0
E = 32
TOP_K = 4
F = 1024
FC = F // P
LIMIT = 7.0
ALPHA = 1.702
EPS = 1e-6
SCALE = HD ** -0.5

SLOTS = 64
MAX_PASSES = E + SEQ * TOP_K // SLOTS - 1
TABLE = MAX_PASSES + 1
UNITS = 12
DOUBLE = 7
UNIT = 2 * F
AHEAD = 24
HALFWAY = E // 2
NOT_ROUTED = -16384.0

C_ID = 0
C_TRI = C_ID + P
C_TRI_IN = C_TRI + P
C_ONE = C_TRI_IN + E
C_IOTA = C_ONE + P
C_COSA = C_IOTA + 2 * SLOTS
C_SINA = C_COSA + TC * HD
C_COSB = C_SINA + TC * HD
C_SINB = C_COSB + TC * HD
C_LOGM = C_SINB + TC * HD
C_END = C_LOGM + TC * SEQ

PROJ = (
    ("qa", 0, 512, 0),
    ("kva", 512, 256, 2),
    ("vb", 1792, 512, 3),
    ("qb", 768, 512, 5),
    ("kb", 1280, 512, 7),
)
PROJ_UNITS = 9
PROJ_BANK = (4, 5, 6, 7, 0, 1, 1, 2, 1, 2)
S_BANK = (3, 4)
PT_BANK = (5, 6)
O_BANK = (7, 0)
OPA_BANK = (1, 2, 1, 2)
OPB_BANK = (5, 6, 7, 0)
PAIRS = tuple((j, j + GROUP_A) for j in range(GROUP_A)) + \
    tuple((HEADS_A + 2 * j, HEADS_A + 2 * j + 1) for j in range(HEADS_B // 2))
A_PAIRS = HEADS_A // 2
Q_SPLIT = 5
SP_BANK = (7, 6, 3, 5)

R_MAX = 3
R_SEL = 14
R_NPASS = 20
R_WT = 22
R_PICK = 28
R_PSUM = 31


def constants():
    c = np.zeros((P, C_END), np.float32)
    c[:, C_ID:C_ID + P] = np.eye(P)
    t = np.arange(P)
    c[:, C_TRI:C_TRI + P] = t[:, None] < t[None, :]
    e = np.arange(E)
    c[:E, C_TRI_IN:C_TRI_IN + E] = e[:, None] <= e[None, :]
    c[:, C_ONE:C_ONE + P] = 1.0
    c[:, C_IOTA:C_IOTA + 2 * SLOTS] = np.arange(2 * SLOTS) % SLOTS
    pos = np.arange(SEQ)

    def angles(at, dim):
        inv = np.float32(THETA) ** (-np.arange(0, dim, 2, dtype=np.float32) / np.float32(dim))
        return at.astype(np.float32)[:, None] * inv[None, :].astype(np.float32)

    row, col, one = angles(pos // GRID_W, HD // 2), angles(pos % GRID_W, HD // 2), angles(pos, HD)
    cos_a = np.concatenate([np.cos(row), np.cos(row), np.cos(col), np.cos(col)], 1)
    sin_a = np.concatenate([-np.sin(row), np.sin(row), -np.sin(col), np.sin(col)], 1)
    cos_b = np.concatenate([np.cos(one), np.cos(one)], 1)
    sin_b = np.concatenate([-np.sin(one), np.sin(one)], 1)
    for at, table in ((C_COSA, cos_a), (C_SINA, sin_a), (C_COSB, cos_b), (C_SINB, sin_b)):
        c[:, at:at + TC * HD] = table.reshape(TC, P, HD).transpose(1, 0, 2).reshape(P, TC * HD)
    delta = pos[None, :] - pos[:, None]
    times = sum(((delta % dil == 0) & (abs(delta) <= window // 2)).astype(np.float32)
                for window, dil in BRANCHES)
    logm = np.where(times > 0, np.log(np.maximum(times, 1.0)), -1e30).astype(np.float32)
    c[:, C_LOGM:C_END] = logm.reshape(TC, P, SEQ).transpose(1, 0, 2).reshape(P, TC * SEQ)
    return c


def encoder_kernel(nc, x, attn_norm, w_in, q_norm, k_norm, out_norm_a, out_norm_b, w_out,
                   ffn_norm, w_router, b_router, w_gate, b_gate, w_up, b_up, w_down, b_down,
                   final_norm, consts, out):
    with ExitStack() as ctx:
        def sb(name, shape, dt=F32):
            return ctx.enter_context(nc.sbuf_tensor(name, shape, dt))

        def sem(name):
            return ctx.enter_context(nc.semaphore(name))

        ring = sb("ring", [P, (UNITS + DOUBLE) * UNIT])
        wout_a = sb("wout_a", [P, KC - 2, D])
        acc = sb("acc", [P, TC, D])
        xs = sb("xs", [P, TC, D])

        def in_unit(u, at, *dims):
            n = int(np.prod(dims))
            v = ring[:, (DOUBLE + u) * UNIT + at:(DOUBLE + u) * UNIT + at + n]
            if len(dims) == 1:
                return v
            if len(dims) == 2:
                return v.rearrange("p (a b) -> p a b", b=dims[1])
            return v.rearrange("p (a b c d) -> p a b c d", b=dims[1], c=dims[2], d=dims[3])

        qr = in_unit(0, 0, TC, HEADS * HD)
        kr = in_unit(1, 0, TC, (KV_A + HEADS_B) * HD)
        rot = in_unit(1, TC * (KV_A + HEADS_B) * HD, 3, 2, TC, HD)
        work = in_unit(2, 0, 4, 512)
        wout_b = in_unit(3, 0, 2, D)
        vv = in_unit(4, 0, TC, (KV_A + HEADS_B) * HD)
        part2 = in_unit(4, TC * (KV_A + HEADS_B) * HD, 512)
        wr = in_unit(4, TC * (KV_A + HEADS_B) * HD + 512, KC, E)
        hT = in_unit(5, 0, KC, SEQ)
        qT_a = sb("qT_a", [P, Q_SPLIT, SEQ])
        qT_b = in_unit(6, 0, HEADS // 2 - Q_SPLIT, SEQ)
        kT = in_unit(6, (HEADS // 2 - Q_SPLIT) * SEQ, (KV_A + HEADS_B) // 2, SEQ)
        masked = hT[:, 4:8, :].rearrange("p (b c) k -> p b c k", b=2)
        cst = sb("cst", [P, C_END])
        vecs = sb("vecs", [3 * KC, P])
        gains = sb("gains", [P, 3 * KC])
        qkg = sb("qkg", [P, 2, HD])
        brt = sb("brt", [P, E])
        bu = cst[0:E, C_COSA:C_COSA + F]
        fgain = cst[:, C_COSA:C_COSA + D]
        wo_flat = wout_a[:, :, :].rearrange("p k n -> p (k n)")
        bg = wo_flat[0:E, 10 * 512:10 * 512 + F]
        bd = bg.rearrange("e (j n) -> e j n", j=2)
        ss = sb("ss", [P, 16])
        ms = sb("ms", [P, 16])
        rsq = sb("rsq", [P, TC])
        nhalf = sb("nhalf", [P, HEADS_A])
        unread = sb("unread", [P, 4])
        rstd = sb("rstd", [P, 16])
        hss = sb("hss", [P, 4, HEADS_A])
        hms = sb("hms", [P, 4, HEADS_A])
        hrp = sb("hrp", [P, 4, HEADS_A])
        hrs = sb("hrs", [P, 4, HEADS_A])
        mx = sb("mx", [P, HEADS, TC])
        nmx = sb("nmx", [P, HEADS, TC])
        rs = sb("rs", [P, TC, HEADS])
        ri = sb("ri", [P, TC, HEADS])
        m8 = sb("m8", [P, TC, 8])
        room = sb("room", [P, TC])
        more = sb("more", [P, TC])
        nv0 = sb("nv0", [P, TC])
        den = sb("den", [P, TC])
        rden = sb("rden", [P, TC])
        npass = sb("npass", [E, 4])
        cum = sb("cum", [E, 2])
        ohA, oh, ohz = (wo_flat[0:E, 9 * 512 + 256 + i * TABLE:9 * 512 + 256 + (i + 1) * TABLE] for i in range(3))
        p64 = sb("p64", [P, TABLE])
        base = sb("base", [P, TABLE])
        slot_p = sb("slot_p", [P, TC, TABLE])
        gate_p = sb("gate_p", [P, TC, TABLE])
        tab = sb("tab", [1, 1 + E], I32)

        q_flat = qT_a[:, :, :].rearrange("p k s -> p (k s)")
        q_flat_b = qT_b.rearrange("p k s -> p (k s)")
        n_bias = 2 * FC * TABLE
        bias_p = q_flat[:, 0:n_bias].rearrange("p (j m q) -> p j m q", j=2, m=FC)
        rT = q_flat[0:E, n_bias:n_bias + 2 * SEQ].rearrange("e (j s) -> e j s", j=2)

        lg, gt, eq, sel, ew, ex, wt, rk, rkc = (
            q_flat_b[:, i * TC * E:(i + 1) * TC * E].rearrange("p (c e) -> p c e", c=TC) for i in range(9))
        at = 9 * TC * E
        n_scan = TC * (E + E // 2)
        scan = q_flat_b[:, at:at + 2 * n_scan].rearrange("p (b c e) -> p b c e", b=2, c=TC)

        def temp(n, size):
            return wo_flat[:, n:n + size]

        xT = temp(0, 512)
        g, sg, u_t, act_t, yrows, grow, urow = (temp(512 * i, 512) for i in range(1, 8))
        xrow = grow
        G = temp(512 * 8, TC * 2 * SLOTS).rearrange("p (c s) -> p c s", s=2 * SLOTS)
        GT = temp(512 * 8 + 256, SEQ)
        S = temp(512 * 9, TC * SLOTS).rearrange("p (c s) -> p c s", s=SLOTS)

        prob = work[:, 0:2, :].rearrange("p b (c k) -> p b c k", c=TC)
        probT = work[:, 2:4, :].rearrange("p b (c k) -> p b c k", c=TC)
        o = xs

        banks = [ctx.enter_context(nc.psum_tensor(f"bank{i}", [P, 512], F32)) for i in range(8)]

        ident = cst[:, C_ID:C_ID + P]
        tri = cst[:, C_TRI:C_TRI + P]
        tri_in = cst[0:E, C_TRI_IN:C_TRI_IN + E]
        ones = cst[:, C_ONE:C_ONE + P]
        iota = cst[:, C_IOTA:C_IOTA + SLOTS]
        iota_twice = cst[:, C_IOTA:C_IOTA + 2 * SLOTS]

        def table(at):
            return cst[:, at:at + TC * HD].rearrange("p (c d) -> p c d", c=TC)

        logm = cst[:, C_LOGM:C_END].rearrange("p (c k) -> p c k", c=TC)

        def unit(u, odd=False):
            at = u if u < DOUBLE and not odd else DOUBLE + u
            return ring[:, at * UNIT:(at + 1) * UNIT]

        x_in = [sem(f"x_in{c}") for c in range(TC)]
        cst_in = sem("cst_in")
        vecs_in = [sem(f"vecs_in{i}") for i in range(4)]
        qkg_in = [sem(f"qkg_in{i}") for i in range(2)]
        proj_in = [sem(f"proj_in{u}") for u in range(PROJ_UNITS)]
        wout_in = [sem(f"wout_in{i}") for i in range(4)]
        wr_in = sem("wr_in")
        brt_in = sem("brt_in")
        bg_in, bu_in, bd_in = sem("bg_in"), sem("bu_in"), sem("bd_in")
        fgain_in = sem("fgain_in")
        unit_in = [sem(f"unit_in{u}") for u in range(UNITS)]
        out_stored = sem("out_stored")
        sq_done = sem("sq_done")
        ms_done = sem("ms_done")
        rstd_done = sem("rstd_done")
        xs_done = sem("xs_done")
        gains_turned, gains_ready = sem("gains_turned"), sem("gains_ready")
        rot_ready = sem("rot_ready")
        x_turned, hT_ready = sem("x_turned"), sem("hT_ready")
        proj_done = sem("proj_done")
        hsq_done, hss_done = sem("hsq_done"), sem("hss_done")
        hms_done, hrp_done, hrs_done = sem("hms_done"), sem("hrp_done"), sem("hrs_done")
        normed = sem("normed")
        rot_parts = sem("rot_parts")
        rope_ready = sem("rope_ready")
        v_ready = sem("v_ready")
        qk_turned = sem("qk_turned")
        qkT_ready = sem("qkT_ready")
        scores_done = sem("scores_done")
        masked_ready = sem("masked_ready")
        mx_ready, nmx_ready = sem("mx_ready"), sem("nmx_ready")
        prob_ready = sem("prob_ready")
        prob_turned = sem("prob_turned")
        probTa_ready, probTb_ready = sem("probTa_ready"), sem("probTb_ready")
        pv_done = sem("pv_done")
        ri_ready = sem("ri_ready")
        o_ready = sem("o_ready")
        ident_in = sem("ident_in")
        nhalf_ready = sem("nhalf_ready")
        oproj_done = sem("oproj_done")
        x1_ready = sem("x1_ready")
        logits_done = sem("logits_done")
        r_step = sem("r_step")
        exp_ready = sem("exp_ready")
        ranks_done, cum_done, turned_done = sem("ranks_done"), sem("cum_done"), sem("turned_done")
        picks_done, biases_done = sem("picks_done"), sem("biases_done")
        bdown_done = sem("bdown_done")
        biasg_ready, biasu_ready = sem("biasg_ready"), sem("biasu_ready")
        p64_ready = sem("p64_ready")
        tab_ready = sem("tab_ready")
        unit_used = [sem(f"unit_used{u}") for u in range(UNITS)]
        gathered, xrow_ready = sem("gathered"), sem("xrow_ready")
        xrow_turned, xT_ready = sem("xrow_turned"), sem("xT_ready")
        S_ready, G_ready = sem("S_ready"), sem("G_ready")
        gate_biased, gate_clamped = sem("gate_biased"), sem("gate_clamped")
        sig_ready, gs_ready = sem("sig_ready"), sem("gs_ready")
        up_biased, up_clamped, act_ready = sem("up_biased"), sem("up_clamped"), sem("act_ready")
        grow_ready, urow_ready = sem("grow_ready"), sem("urow_ready")
        gate_turned, up_turned = sem("gate_turned"), sem("up_turned")
        G_turned, GT_ready = sem("G_turned"), sem("GT_ready")
        yrows_ready = sem("yrows_ready")
        spread = [sem(f"spread{i}") for i in range(4)]
        added = [sem(f"added{i}") for i in range(4)]
        bias_added = sem("bias_added")
        fin_ready = sem("fin_ready")

        block = ctx.enter_context(nc.Block())

        w_by_unit = [(w, 2 * j) for w in (w_gate, w_up, w_down) for j in range(4)]

        def load_unit(sp, u, e, odd=False):
            w, k = w_by_unit[u]
            src = w[0, e, k * P:(k + 2) * P, :] if isinstance(e, int) else \
                w[0, bass.ds(e, 1), k * P:(k + 2) * P, :].rearrange("e r n -> (e r) n")
            sp.dma_start(unit(u, odd).rearrange("p (k n) -> p k n", k=2),
                         src.rearrange("(k p) n -> p k n", p=P)).then_inc(unit_in[u], 16)

        @block.sync
        def _(sp):
            sp.dma_start(cst[:, 0:P], consts[:, 0:P]).then_inc(ident_in, 16)
            for c in range(TC):
                sp.dma_start(acc[:, c, :], x[0, c * P:(c + 1) * P, :]).then_inc(x_in[c], 16)
            for _, col, width, u0 in PROJ:
                rows = UNIT // width
                for j in range(KC // rows):
                    sp.dma_start(
                        unit(u0 + j).rearrange("p (k n) -> p k n", n=width),
                        w_in[0, j * rows * P:(j + 1) * rows * P, col:col + width]
                        .rearrange("(k p) n -> p k n", p=P)).then_inc(proj_in[u0 + j], 16)
                if u0 == 0:
                    sp.dma_start(cst[:, P:], consts[:, P:]).then_inc(cst_in, 16)
            for i in range(4):
                sp.dma_start(wout_a[:, 2 * i:2 * i + 2, :] if i < 3 else wout_b,
                             w_out[0, 2 * i * P:2 * (i + 1) * P, :]
                             .rearrange("(k p) n -> p k n", p=P)).then_inc(wout_in[i], 16)
            for u in range(PROJ_UNITS, UNITS):
                load_unit(sp, u, 0)
            for g, (_, _, width, u0) in enumerate(PROJ):
                sp.wait_ge(proj_done, 2 * g + 2)
                for j in range(KC * width // UNIT):
                    load_unit(sp, u0 + j, 0)
            for u, (read, n) in enumerate(((qk_turned, 7), (qk_turned, 7), (pv_done, len(PAIRS)), (oproj_done, 8),
                                           (logits_done, 1), (logits_done, 1), (r_step, R_PSUM))):
                sp.wait_ge(read, n)
                sp.wait_ge(unit_in[u], 16)
                load_unit(sp, u, 1, odd=True)
            sp.wait_ge(tab_ready, 1)

            def last_units(e, upto):
                for u in range(DOUBLE, UNITS):
                    sp.wait_ge(unit_in[u], 16)
                    sp.wait_ge(unit_used[u], upto)
                    load_unit(sp, u, e)

            def first_units(e, odd, upto, landed):
                for u in range(DOUBLE):
                    sp.wait_ge(unit_in[u], 32)
                    sp.wait_ge(unit_used[u], upto)
                    sp.wait_ge(unit_in[u], landed)
                    load_unit(sp, u, e, odd)

            def passes_upto(e):
                at = slice(e + 1, e + 2) if isinstance(e, int) else bass.ds(e + 1, 1)
                return sp.value_load(tab[0:1, at], min_val=1, max_val=MAX_PASSES)

            with sp.Fori(0, AHEAD // 2) as pair:
                for odd in (False, True):
                    e = pair * 2 + int(odd)
                    upto = passes_upto(e)
                    first_units(e + 2, odd, upto, sp.snap(e * 16 + 32))
                    last_units(e + 1, upto)
            last_units(AHEAD + 1, passes_upto(AHEAD))
            with sp.Fori(0, (E - AHEAD - 4) // 2) as pair:
                for odd in (False, True):
                    e = pair * 2 + (AHEAD + 2 + int(odd))
                    first_units(e, odd, passes_upto(e - 2), sp.snap(e * 16))
                    last_units(e, passes_upto(e - 1))
            sp.wait_ge(bdown_done, 4)
            sp.dma_start(fgain, final_norm.rearrange("(a d) -> a d", a=1).broadcast_to([P, D])).then_inc(fgain_in, 16)
            for e in range(E - 2, E):
                first_units(e, e % 2 == 1, passes_upto(e - 2), 16 * e)
                last_units(e, passes_upto(e - 1))
            for c in range(TC):
                sp.wait_ge(fin_ready, c + 1)
                sp.dma_start(out[0, c * P:(c + 1) * P, :], xs[:, c, :]).then_inc(out_stored, 16)
            sp.wait_ge(out_stored, 16 * TC)

        @block.gpsimd
        def _(pool):
            pool.memset(nhalf[:, :], -0.5).then_inc(nhalf_ready, 1)
            for i in range(4):
                pool.memset(unread[:, i:i + 1], 0.0).then_inc(added[i], 1)
            pool.wait_ge(nhalf_ready, 1)

            def norms(n, n_sq, a, width, chunks=TC):
                b = a + chunks
                pool.wait_ge(sq_done, n_sq)
                pool.tensor_scalar(ms[:, a:b], ss[:, a:b], 1.0 / width, EPS, ALU.mult, ALU.add).then_inc(ms_done, 1)
                pool.wait_ge(ms_done, n)
                pool.tensor_tensor(rstd[:, a:b], ms[:, a:b], nhalf[:, 0:chunks], ALU.pow).then_inc(rstd_done, 1)

            norms(1, 2, 0, D)
            pool.wait_ge(rstd_done, 1)
            pool.tensor_tensor(rsq[:, :], rstd[:, 0:2], rstd[:, 0:2], ALU.mult).then_inc(hms_done, 1)
            pool.wait_ge(hms_done, 1)
            for i, heads in enumerate((HEADS_A, HEADS_A, KV_A, KV_A)):
                c = i % 2
                pool.wait_ge(hss_done, i + 1)
                pool.tensor_scalar(hms[:, i, 0:heads], hss[:, i, 0:heads], rsq[:, c:c + 1], None, ALU.mult)\
                    .then_inc(hms_done, 1)
                pool.wait_ge(hms_done, 2 * i + 2)
                pool.tensor_scalar(hms[:, i, 0:heads], hms[:, i, 0:heads], 1.0 / HD, EPS, ALU.mult, ALU.add)\
                    .then_inc(hms_done, 1)
                pool.wait_ge(hms_done, 2 * i + 3)
                pool.tensor_tensor(hrp[:, i, 0:heads], hms[:, i, 0:heads], nhalf[:, 0:heads], ALU.pow)\
                    .then_inc(hrp_done, 1)
                pool.wait_ge(hrp_done, i + 1)
                pool.tensor_scalar(hrs[:, i, 0:heads], hrp[:, i, 0:heads], rstd[:, c:c + 1], None, ALU.mult)\
                    .then_inc(hrs_done, 1)
            norms(2, 4, 2, 512)
            pool.wait_ge(cst_in, 16)
            pool.tensor_scalar(p64[:, :], iota[:, 0:TABLE], float(SLOTS), 0.0, ALU.mult, ALU.add)\
                .then_inc(p64_ready, 1)
            norms(3, 6, 4, 512)
            norms(4, 8, 6, D)
            norms(5, 9, 8, D, 1)
            norms(6, 10, 9, D, 1)

        @block.scalar
        def _(act):
            for i, (v, a, n) in enumerate(((attn_norm, 0, KC), (ffn_norm, KC, KC),
                                           (out_norm_a, 2 * KC, KC // 2),
                                           (out_norm_b, 2 * KC + KC // 2, KC // 2))):
                act.dma_start(vecs[a:a + n, :], v[0, :].rearrange("(k p) -> k p", p=P)).then_inc(vecs_in[i], 16)
            for i, v in enumerate((q_norm, k_norm)):
                act.dma_start(qkg[:, i, :], v.broadcast_to([P, HD])).then_inc(qkg_in[i], 16)

            def sum_squares(src, junk, col):
                act.activation(junk, src, ACT.Square, accum_out=ss[:, col:col + 1]).then_inc(sq_done, 1)

            for c in range(TC):
                act.wait_ge(x_in[c], 16)
                sum_squares(acc[:, c, :], xs[:, c, :], c)
            act.dma_start(wr[:, :, :], w_router[0].rearrange("(k p) e -> p k e", p=P)).then_inc(wr_in, 16)
            act.dma_start(brt[:, :], b_router.broadcast_to([P, E])).then_inc(brt_in, 16)

            for i, heads in enumerate((HEADS_A, HEADS_A, KV_A, KV_A)):
                act.wait_ge(proj_done, i + 1)
                w = heads * HD
                if i >= 1:
                    act.wait_ge(hss_done, i)
                act.activation(work[:, 3, 0:w], banks[PROJ_BANK[i]][:, 0:w], ACT.Square).then_inc(hsq_done, 1)
                if i == 2:
                    act.wait_ge(rstd_done, 1)
                if i >= 2:
                    act.activation(vv[:, i % 2, 0:KV_A * HD], banks[PROJ_BANK[i]][:, w:2 * w], ACT.Copy,
                                   scale=rstd[:, i % 2:i % 2 + 1]).then_inc(v_ready, 1)
            for i in (4, 5):
                act.wait_ge(proj_done, i + 1)
                act.activation(vv[:, i % 2, KV_A * HD:], banks[PROJ_BANK[i]][:, :], ACT.Copy,
                               scale=rstd[:, i % 2:i % 2 + 1]).then_inc(v_ready, 1)

            def qk_copy(n):
                dsts, bank = (((qT_a[:, 0:2, :],), 2), ((qT_a[:, 2:4, :],), 3), ((kT[:, 0:1, :],), 4),
                              ((qT_a[:, 4:5, :], qT_b[:, 0:1, :]), 2), ((qT_b[:, 1:3, :],), 3),
                              ((kT[:, 1:3, :],), 1), ((kT[:, 3:5, :],), 2))[n]
                act.wait_ge(qk_turned, n + 1)
                at = 0
                for dst in dsts:
                    w = dst.shape[1] * SEQ
                    last = act.activation(dst.rearrange("p k s -> p (k s)"), banks[bank][:, at:at + w], ACT.Copy)
                    at += w
                last.then_inc(qkT_ready, 1)

            for n in range(3):
                qk_copy(n)

            def exps(i, j):
                h = PAIRS[i][j]
                act.wait_ge(nmx_ready, 2 * i + j + 1)
                if i >= 1:
                    act.wait_ge(prob_turned, 2 * i - 1 + j)
                for c in range(TC):
                    src = banks[S_BANK[j]][:, c * SEQ:(c + 1) * SEQ] if i < A_PAIRS else masked[:, j, c, :]
                    last = act.activation(prob[:, j, c, :], src, ACT.Exp, bias=nmx[:, h, c:c + 1],
                                          scale=SCALE if i < A_PAIRS else 1.0, accum_out=rs[:, c, h:h + 1])
                last.then_inc(prob_ready, 1)

            def squares_of_outputs(half):
                act.wait_ge(o_ready, 4 * half + 4)
                for c in range(TC):
                    if half or c:
                        act.wait_ge(sq_done, 2 + 2 * half + c)
                    sum_squares(o[:, c, half * 512:(half + 1) * 512], part2[:, :], 2 + 2 * half + c)

            for i in range(len(PAIRS)):
                if i == A_PAIRS:
                    qk_copy(5)
                    qk_copy(6)
                    squares_of_outputs(0)
                exps(i, 0)
                exps(i, 1)
                act.wait_ge(prob_turned, 2 * i + 2)
                if i >= 1:
                    act.wait_ge(pv_done, i)
                act.activation(probT[:, 1, :, :].rearrange("p c k -> p (c k)"), banks[PT_BANK[1]][:, :],
                               ACT.Copy).then_inc(probTb_ready, 1)
                if i == A_PAIRS - 2:
                    qk_copy(3)
                    qk_copy(4)

            squares_of_outputs(1)
            act.dma_start(bu, b_up[0]).then_inc(bu_in, 16)
            act.wait_ge(oproj_done, 8)
            act.dma_start(bg, b_gate[0]).then_inc(bg_in, 16)
            for c in range(TC):
                act.wait_ge(x1_ready, 6 + 2 * c)
                sum_squares(acc[:, c, :], (qT_a, kT)[c][:, 0:4, :].rearrange("p k s -> p (k s)"), 6 + c)

            act.wait_ge(r_step, R_MAX)
            for c in range(TC):
                last = act.activation(ex[:, c, :], lg[:, c, :], ACT.Exp, bias=nv0[:, c:c + 1])
            last.then_inc(exp_ready, 1)
            for c in range(TC):
                act.activation(xs[:, c, :], acc[:, c, :], ACT.Copy, scale=rstd[:, 6 + c:7 + c]).then_inc(xs_done, 1)
            act.wait_ge(tab_ready, 1)
            passes = act.value_load(tab[0:1, E:1 + E], min_val=1, max_val=MAX_PASSES)

            def one_pass(p, first):
                act.wait_ge(unit_used[3], p + 1)
                if not first:
                    act.wait_ge(gate_turned, p)
                act.activation(grow, banks[1][:, :], ACT.Copy).then_inc(grow_ready, 1)
                act.wait_ge(gate_clamped, p + 1)
                act.activation(sg, g, ACT.Sigmoid, scale=ALPHA).then_inc(sig_ready, 1)
                if first:
                    act.wait_ge(biases_done, 1)
                    act.dma_start(bd, b_down[0].rearrange("e (j n) -> e j n", j=2)).then_inc(bd_in, 16)
                    act.wait_ge(biases_done, 2)
                    act.activation(bias_p[:, 1, :, :].rearrange("p m q -> p (m q)"), banks[7][:, 0:FC * TABLE],
                                   ACT.Copy).then_inc(biasu_ready, 1)
                act.wait_ge(unit_used[7], p + 1)
                act.activation(urow, banks[2][:, :], ACT.Copy).then_inc(urow_ready, 1)
                act.wait_ge(G_turned, p + 1)
                act.activation(GT, banks[6][:, 0:SEQ], ACT.Copy).then_inc(GT_ready, 1)
                rows_out(p + 2)
                act.wait_ge(unit_used[UNITS - 1], p + 1)
                act.activation(yrows, banks[3][:, :], ACT.Copy).then_inc(yrows_ready, 1)

            def rows_out(n):
                act.wait_ge(gathered, n)
                act.activation(xrow, banks[0][:, :], ACT.Copy).then_inc(xrow_ready, 1)

            rows_out(1)
            one_pass(0, True)
            with act.Fori(1, passes) as p:
                one_pass(p, False)

            for c in range(TC):
                act.wait_ge(added[2 * c], passes + 1)
                act.wait_ge(added[2 * c + 1], passes + 1)
                sum_squares(acc[:, c, :], wo_flat[:, c * D:(c + 1) * D], 8 + c)

        @block.tensor
        def _(pe):
            pe.wait_ge(ident_in, 16)
            for i in range(4):
                pe.wait_ge(vecs_in[i], 16)
            pe.transpose(banks[7][:, 0:3 * KC], vecs[:, :], ident[0:3 * KC, 0:3 * KC]).then_inc(gains_turned, 1)

            def turn_rows(src, bank_of, chunks=range(KC)):
                for n, k in enumerate(chunks):
                    for c in range(TC):
                        last = pe.transpose(banks[bank_of[n // 2]][:, k % 2 * SEQ + c * P:k % 2 * SEQ + (c + 1) * P],
                                            src[:, c, k * P:(k + 1) * P], ident)
                    if k % 2:
                        last.then_inc(x_turned, 1)

            for c in range(TC):
                pe.wait_ge(x_in[c], 16)
            turn_rows(acc, (0, 1, 2, 3))

            def project(i):
                _, _, width, u0 = PROJ[i // 2]
                c, rows = i % 2, UNIT // width
                if i == 3:
                    pe.wait_ge(gains_ready, 1)
                if i == 6:
                    pe.wait_ge(v_ready, 4)
                if i == 8:
                    pe.wait_ge(rope_ready, 5)
                if i == 9:
                    pe.wait_ge(rope_ready, 6)
                    pe.wait_ge(qkT_ready, 4)
                for k in range(KC):
                    if c == 0:
                        pe.wait_ge(proj_in[u0 + k // rows], 16)
                    if i == 0:
                        pe.wait_ge(hT_ready, k // 2 + 1)
                    last = pe.matmul(banks[PROJ_BANK[i]][:, 0:width], hT[:, k, c * P:(c + 1) * P],
                                     unit(u0 + k // rows)[:, (k % rows) * width:(k % rows + 1) * width],
                                     start=(k == 0), stop=(k == KC - 1))
                last.then_inc(proj_done, 1)

            def turn_pairs(src, pairs, bank):
                for n, pair in enumerate(pairs):
                    for c in range(TC):
                        last = pe.transpose(banks[bank][:, n * SEQ + c * P:n * SEQ + (c + 1) * P],
                                            src[:, c, pair * P:(pair + 1) * P], ident)
                last.then_inc(qk_turned, 1)

            for i in range(6):
                project(i)
            pe.wait_ge(rope_ready, 4)
            turn_pairs(qr, (0, 1), 2)
            turn_pairs(qr, (2, 3), 3)
            turn_pairs(kr, (0,), 4)

            def scores(i):
                kpair = 0 if i < A_PAIRS else 1 + i - A_PAIRS
                pe.wait_ge(qkT_ready, 3 if i < A_PAIRS - 1 else 5 if i < A_PAIRS else 7)
                if i >= 1:
                    pe.wait_ge(prob_ready, 2 * i)
                for c in range(TC):
                    for j in range(2):
                        half = slice(j * HD, (j + 1) * HD)
                        queries = qT_a[half, i] if i < Q_SPLIT else qT_b[half, i - Q_SPLIT]
                        last = pe.matmul(banks[S_BANK[j]][:, c * SEQ:(c + 1) * SEQ], queries[:, c * P:(c + 1) * P],
                                         kT[half, kpair, :], start=True, stop=True)
                last.then_inc(scores_done, 1)

            def turn_probs(i):
                for j in range(2):
                    pe.wait_ge(prob_ready, 2 * i + j + 1)
                    if i >= 1:
                        pe.wait_ge(probTa_ready if j == 0 else probTb_ready, i)
                    for kc in range(TC):
                        for c in range(TC):
                            last = pe.transpose(banks[PT_BANK[j]][:, kc * SEQ + c * P:kc * SEQ + (c + 1) * P],
                                                prob[:, j, c, kc * P:(kc + 1) * P], ident)
                    last.then_inc(prob_turned, 1)

            def weigh_values(i):
                if i >= 2:
                    pe.wait_ge(o_ready, i - 1)
                for j, h in enumerate(PAIRS[i]):
                    pe.wait_ge(probTa_ready if j == 0 else probTb_ready, i + 1)
                    vh = h // GROUP_A if h < HEADS_A else KV_A + h - HEADS_A
                    for c in range(TC):
                        for kc in range(TC):
                            last = pe.matmul(banks[O_BANK[i % 2]][:, c * P + j * HD:c * P + (j + 1) * HD],
                                             probT[:, j, kc, c * P:(c + 1) * P], vv[:, kc, vh * HD:(vh + 1) * HD],
                                             start=(kc == 0), stop=(kc == TC - 1))
                last.then_inc(pv_done, 1)

            def project_out(half, i):
                c, n = i // 2, i % 2
                if half == 0 and i >= 2:
                    pe.wait_ge(x1_ready, i - 1)
                for k in range(4 * half, 4 * half + 4):
                    pe.wait_ge(hT_ready, 4 + k // 2 + 1)
                    if i == 0:
                        pe.wait_ge(wout_in[k // 2], 16)
                    last = pe.matmul(banks[(OPA_BANK, OPB_BANK)[half][i]][:, :], hT[:, k, c * P:(c + 1) * P],
                                     (wout_a[:, k] if k < KC - 2 else wout_b[:, k - KC + 2])[:, n * 512:(n + 1) * 512],
                                     start=(k % 4 == 0), stop=(k % 4 == 3))
                last.then_inc(oproj_done, 1)

            for i in range(A_PAIRS):
                scores(i)
                if i >= 1:
                    weigh_values(i - 1)
                project(6 + i)
                turn_probs(i)
                if i == A_PAIRS - 2:
                    pe.wait_ge(rope_ready, 6)
                    turn_pairs(qr, (4, 5), 2)
                    turn_pairs(qr, (6, 7), 3)
            weigh_values(A_PAIRS - 1)
            pe.wait_ge(rope_ready, 8)
            turn_pairs(kr, (1, 2), 1)
            turn_pairs(kr, (3, 4), 2)
            pe.wait_ge(o_ready, A_PAIRS)
            pe.wait_ge(qkT_ready, 7)
            turn_rows(o, (1, 2), range(0, 4))
            for i in range(A_PAIRS, len(PAIRS)):
                scores(i)
                if i > A_PAIRS:
                    weigh_values(i - 1)
                project_out(0, i - A_PAIRS)
                turn_probs(i)
            weigh_values(len(PAIRS) - 1)
            pe.wait_ge(o_ready, len(PAIRS))
            turn_rows(o, (3, 4), range(4, 8))
            for i in range(4):
                project_out(1, i)

            pe.wait_ge(x1_ready, 8)
            turn_rows(acc, (1, 2, 3, 4))
            pe.wait_ge(wr_in, 16)
            for c in range(TC):
                for k in range(KC):
                    pe.wait_ge(hT_ready, 8 + k // 2 + 1)
                    last = pe.matmul(banks[5][:, c * E:(c + 1) * E], hT[:, k, c * P:(c + 1) * P], wr[:, k, :],
                                     start=(k == 0), stop=(k == KC - 1))
            last.then_inc(logits_done, 1)
            pe.wait_ge(cst_in, 16)
            pe.wait_ge(r_step, R_SEL)
            pe.matmul(banks[6][:, 0:E], tri, sel[:, 0, :], start=True, stop=True)
            pe.matmul(banks[6][:, E:2 * E], tri, sel[:, 1, :], start=True, stop=False)
            pe.matmul(banks[6][:, E:2 * E], ones, sel[:, 0, :], start=False, stop=True)
            pe.matmul(banks[6][0:E, 2 * E:2 * E + 1], sel[:, 0, :], ones[:, 0:1], start=True, stop=False)
            pe.matmul(banks[6][0:E, 2 * E:2 * E + 1], sel[:, 1, :], ones[:, 0:1], start=False, stop=True)\
              .then_inc(ranks_done, 1)
            pe.wait_ge(r_step, R_NPASS)
            pe.matmul(banks[0][0:E, 0:1], tri_in, npass[:, 3:4], start=True, stop=True).then_inc(cum_done, 1)
            pe.wait_ge(r_step, R_WT)
            for c in range(TC):
                pe.transpose(banks[1][0:E, c * P:(c + 1) * P], rkc[:, c, :], ident)
                last = pe.transpose(banks[1][0:E, SEQ + c * P:SEQ + (c + 1) * P], wt[:, c, :], ident)
            last.then_inc(turned_done, 1)
            pe.wait_ge(r_step, R_PICK)
            pe.matmul(banks[2][0:1, 0:1], ones[0:1, 0:1], ones[0:1, 0:1], start=True, stop=True)
            pe.matmul(banks[2][0:1, 1:1 + E], cum[:, 0:1], ident[0:E, 0:E], start=True, stop=True)
            pe.matmul(banks[2][:, 128:128 + TABLE], ones[0:E, :], ohz[:, :], start=True, stop=True)
            for c in range(TC):
                for j in range(2):
                    at = 192 + (2 * j + c) * TABLE
                    last = pe.matmul(banks[2][:, at:at + TABLE], rT[:, j, c * P:(c + 1) * P], oh[:, :],
                                     start=True, stop=True)
            last.then_inc(picks_done, 1)
            pe.wait_ge(tab_ready, 1)

            def passes_upto(e):
                at = slice(e + 1, e + 2) if isinstance(e, int) else bass.ds(e + 1, 1)
                return pe.value_load(tab[0:1, at], min_val=1, max_val=MAX_PASSES)

            pe.wait_ge(xs_done, TC)

            def gather(n):
                pe.wait_ge(S_ready, n)
                for c in range(TC):
                    for half in range(2):
                        last = pe.matmul(banks[0][half * SLOTS:(half + 1) * SLOTS, :], S[:, c, :],
                                         xs[:, c, half * 512:(half + 1) * 512], start=(c == 0), stop=(c == TC - 1))
                last.then_inc(gathered, 1)

            def product(bank, src, units, landed, odd=False):
                for u in units:
                    pe.wait_ge(unit_in[u], landed)
                    for kk in range(2):
                        k = 2 * (u % 4) + kk
                        for half in range(2):
                            at = kk * F + half * 512
                            last = pe.matmul(banks[bank][half * SLOTS:(half + 1) * SLOTS, :], src(k),
                                             unit(u, odd)[:, at:at + 512], start=(k == 0), stop=(k == KC - 1))
                    last.then_inc(unit_used[u], 1)

            def turn(bank, src, done):
                for m in range(FC // 2):
                    last = pe.transpose(banks[bank][:, m * P:(m + 1) * P], src[:, m * P:(m + 1) * P], ident)
                last.then_inc(done, 1)

            def turn_slots(p, first):
                if not first:
                    pe.wait_ge(added[1], p + 1)
                pe.wait_ge(G_ready, p + 1)
                for c in range(TC):
                    last = pe.transpose(banks[6][:, c * P:(c + 1) * P], G[:, c, :], ident)
                last.then_inc(G_turned, 1)

            def spread_results(p, tiles):
                pe.wait_ge(GT_ready, p)
                pe.wait_ge(yrows_ready, p)
                pe.wait_ge(up_biased, p)
                for i in tiles:
                    c, n = i // 2, i % 2
                    pe.wait_ge(added[i], p)
                    half = slice(n * SLOTS, (n + 1) * SLOTS)
                    pe.matmul(banks[SP_BANK[i]][:, :], GT[half, c * P:(c + 1) * P], yrows[half, :],
                              start=True, stop=True).then_inc(spread[i], 1)

            def biases(j, b, landed):
                pe.wait_ge(landed, 16)
                for m in range(FC):
                    last = pe.matmul(banks[3 if j == 0 else 7][:, m * TABLE:(m + 1) * TABLE],
                                     b[:, m * P:(m + 1) * P], oh[:, :], start=True, stop=True)
                last.then_inc(biases_done, 1)

            def down_biases(p):
                pe.wait_ge(bd_in, 16)
                pe.wait_ge(added[0], p)
                pe.wait_ge(GT_ready, p)
                pe.wait_ge(yrows_ready, p)
                pe.wait_ge(up_biased, p)
                for c in range(TC):
                    for n in range(2):
                        pe.matmul(banks[SP_BANK[2 * c + n]][:, :], rT[:, 1, c * P:(c + 1) * P], bd[:, n, :],
                                  start=True, stop=True).then_inc(bdown_done, 1)
                pe.wait_ge(bias_added, 4)

            def one_pass(p, first, landed, odd, last=False):
                pe.wait_ge(xT_ready, p + 1)
                if not first:
                    pe.wait_ge(grow_ready, p)
                product(1, lambda k: xT[:, act_at(k):act_at(k) + SLOTS], range(0, 4), landed, odd)
                if last:
                    spread_results(p, (1, 2, 3))
                if first:
                    biases(0, bg, bg_in)
                else:
                    pe.wait_ge(urow_ready, p)
                    pe.wait_ge(gate_biased, p)
                if not last:
                    product(2, lambda k: xT[:, act_at(k):act_at(k) + SLOTS], range(4, 6), landed, odd)
                pe.wait_ge(grow_ready, p + 1)
                turn(4, grow, gate_turned)
                if last:
                    product(2, lambda k: xT[:, act_at(k):act_at(k) + SLOTS], range(4, 6), landed, odd)
                elif first:
                    biases(1, bu, bu_in)
                else:
                    spread_results(p, (1, 2, 3))
                product(2, lambda k: xT[:, act_at(k):act_at(k) + SLOTS], range(6, 8), landed, odd)
                if not first:
                    spread_results(p, (0,))
                turn_slots(p, first)
                if not first:
                    pe.wait_ge(added[3], p + 1)
                pe.wait_ge(urow_ready, p + 1)
                turn(5, urow, up_turned)
                gather(p + 2)
                pe.wait_ge(act_ready, p + 1)
                if first:
                    pe.wait_ge(biasg_ready, 1)
                else:
                    pe.wait_ge(added[2], p + 1)
                product(3, lambda k: act_t[:, act_at(k):act_at(k) + SLOTS], range(8, 10), landed)
                pe.wait_ge(xrow_ready, p + 2)
                turn(0, xrow, xrow_turned)
                product(3, lambda k: act_t[:, act_at(k):act_at(k) + SLOTS], range(10, 12), landed)

            def act_at(k):
                return (k % 4) * 2 * SLOTS + (k // 4) * SLOTS

            gather(1)
            pe.wait_ge(xrow_ready, 1)
            turn(0, xrow, xrow_turned)
            one_pass(0, True, 16, False)

            def experts(pair, last=False):
                for odd in (False, True):
                    e = pair * 2 + int(odd)
                    landed = 16 * e + 16 if last else pe.snap(e * 16 + 16)
                    start, end = passes_upto(e - 1), passes_upto(e)
                    if odd or last:
                        with pe.Fori(start, end) as p:
                            one_pass(p, False, landed, odd, last)
                    else:
                        with pe.If(end > start):
                            with pe.Fori(start, end) as p:
                                one_pass(p, False, landed, odd)

            with pe.Fori(0, HALFWAY // 2) as pair:
                experts(pair)
            down_biases(passes_upto(HALFWAY - 1))
            with pe.Fori(HALFWAY // 2, E // 2 - 1) as pair:
                experts(pair)
            experts(E // 2 - 1, last=True)
            passes = passes_upto(E - 1)
            spread_results(passes, range(4))

        @block.vector
        def _(dve):
            dve.wait_ge(gains_turned, 1)
            dve.tensor_copy(gains[:, :], banks[7][:, 0:3 * KC]).then_inc(gains_ready, 1)
            dve.wait_ge(gains_ready, 1)

            def scaled_rows(n, bank_of, col, chunks=range(0, KC, 2)):
                for j, k in enumerate(chunks):
                    dve.wait_ge(x_turned, n + j + 1)
                    g = gains[:, col + k:col + k + 2].unsqueeze(2).broadcast_to([P, 2, SEQ])
                    dve.tensor_tensor(hT[:, k:k + 2, :],
                                      banks[bank_of[j]][:, :].rearrange("p (k s) -> p k s", k=2), g, ALU.mult)\
                       .then_inc(hT_ready, 1)

            scaled_rows(0, (0, 1, 2, 3), 0)

            dve.wait_ge(cst_in, 16)
            for i in range(2):
                dve.wait_ge(qkg_in[i], 16)
                for c in range(TC):
                    dve.tensor_tensor(rot[:, i, 0, c, :], table(C_COSA)[:, c, :], qkg[:, i, :], ALU.mult)
                    for a, b in ((0, 16), (16, 0), (32, 48), (48, 32)):
                        last = dve.tensor_tensor(rot[:, i, 1, c, a:a + 16], table(C_SINA)[:, c, a:a + 16],
                                                 qkg[:, i, b:b + 16], ALU.mult)
            dve.wait_ge(rstd_done, 1)
            for c in range(TC):
                for j, at in enumerate((C_COSB, C_SINB)):
                    last = dve.tensor_scalar(rot[:, 2, j, c, :], table(at)[:, c, :], rstd[:, c:c + 1], None, ALU.mult)
            last.then_inc(rot_ready, 1)
            dve.wait_ge(rot_ready, 1)

            def bc(t, heads):
                return t.unsqueeze(1).broadcast_to([P, heads, t.shape[-1]])

            n_rope = 0

            def rotate(src, dst, view, heads, half, cos, sin):
                nonlocal n_rope
                n_rope += 1
                t2 = part2[:, 0:heads * HD]
                if n_rope > 1:
                    dve.wait_ge(rope_ready, n_rope - 1)
                dve.tensor_tensor(dst, view(src), view_bc(view, cos, heads), ALU.mult)
                for at in range(0, HD, half):
                    other = at + half if at // half % 2 == 0 else at - half
                    last = dve.tensor_tensor(
                        t2.rearrange("p (h d) -> p h d", d=HD)[:, :, at:at + half],
                        src.rearrange("p (h d) -> p h d", d=HD)[:, :, other:other + half],
                        bc(sin[:, at:at + half], heads), ALU.mult)
                last.then_inc(rot_parts, 1)
                dve.wait_ge(rot_parts, n_rope)
                dve.tensor_tensor(dst, dst, view(t2), ALU.add).then_inc(rope_ready, 1)

            def view_bc(view, t, heads):
                if view is by_head:
                    return bc(t, heads)
                return t.unsqueeze(1).unsqueeze(1).broadcast_to([P, 2, heads // 2, HD])

            def by_head(t):
                return t.rearrange("p (h d) -> p h d", d=HD)

            def by_pair(t):
                return t.rearrange("p (two j d) -> p two j d", two=2, d=HD)

            for i, heads in enumerate((HEADS_A, HEADS_A, KV_A, KV_A)):
                c, is_k = i % 2, i // 2
                w = heads * HD
                dve.wait_ge(hsq_done, i + 1)
                dve.tensor_reduce(hss[:, i, 0:heads], by_head(work[:, 3, 0:w]), AX.X, ALU.add).then_inc(hss_done, 1)
                dve.wait_ge(hss_done, i + 1)
                dve.wait_ge(hrs_done, i + 1)
                if is_k:
                    dve.wait_ge(v_ready, c + 1)
                t0 = work[:, 2, 0:w]
                dve.tensor_tensor(by_head(t0), by_head(banks[PROJ_BANK[i]][:, 0:w]),
                                  hrs[:, i, 0:heads].unsqueeze(2).broadcast_to([P, heads, HD]), ALU.mult)\
                   .then_inc(normed, 1)
                dve.wait_ge(normed, i + 1)
                if is_k:
                    rotate(t0, by_head(kr[:, c, 0:w]), by_head, heads, 16, rot[:, 1, 0, c, :], rot[:, 1, 1, c, :])
                else:
                    dst = qr[:, c, 0:w].rearrange("p (j two d) -> p two j d", two=2, d=HD)
                    rotate(t0, dst, by_pair, heads, 16, rot[:, 0, 0, c, :], rot[:, 0, 1, c, :])

            def rotate_b(i):
                c = i % 2
                dve.wait_ge(proj_done, i + 1)
                dst = qr[:, c, HEADS_A * HD:] if i < 8 else kr[:, c, KV_A * HD:]
                rotate(banks[PROJ_BANK[i]][:, :], by_head(dst), by_head, HEADS_B, 32, rot[:, 2, 0, c, :], rot[:, 2, 1, c, :])

            def row_max(i, j):
                h, n = PAIRS[i][j], 2 * i + j
                dve.wait_ge(scores_done, i + 1)
                src = banks[S_BANK[j]][:, :].rearrange("p (c k) -> p c k", c=TC)
                if i < A_PAIRS:
                    dve.tensor_reduce(mx[:, h, :], src, AX.X, ALU.max).then_inc(mx_ready, 1)
                    dve.wait_ge(mx_ready, n + 1)
                    dve.tensor_scalar(nmx[:, h, :], mx[:, h, :], -SCALE, None, ALU.mult).then_inc(nmx_ready, 1)
                else:
                    if i > A_PAIRS:
                        dve.wait_ge(prob_ready, n - 1)
                    dve.scalar_tensor_tensor(out=masked[:, j, :, :], in0=src, scalar=SCALE, in1=logm,
                                             op0=ALU.mult, op1=ALU.add).then_inc(masked_ready, 1)
                    dve.wait_ge(masked_ready, n - 2 * A_PAIRS + 1)
                    dve.tensor_reduce(nmx[:, h, :], masked[:, j, :, :], AX.X, ALU.max, negate=True)\
                       .then_inc(nmx_ready, 1)

            def outputs_of(i):
                step = PAIRS[i][1] - PAIRS[i][0]
                h0 = PAIRS[i][0]
                heads = slice(h0, h0 + step + 1, step)
                dve.wait_ge(prob_ready, 2 * i + 2)
                dve.reciprocal(ri[:, :, heads], rs[:, :, heads]).then_inc(ri_ready, 1)
                dve.wait_ge(ri_ready, i + 1)
                dve.wait_ge(pv_done, i + 1)
                for c in range(TC):
                    last = dve.tensor_tensor(by_head(o[:, c, :])[:, heads, :],
                                             by_head(banks[O_BANK[i % 2]][:, c * P:(c + 1) * P]),
                                             ri[:, c, heads].unsqueeze(2).broadcast_to([P, 2, HD]), ALU.mult)
                last.then_inc(o_ready, 1)

            def onto_stream(half, i):
                c, n = i // 2, i % 2
                part = acc[:, c, n * 512:(n + 1) * 512]
                dve.wait_ge(rstd_done, 2 + half)
                dve.wait_ge(oproj_done, 4 * half + i + 1)
                if half:
                    dve.wait_ge(x1_ready, i + 1)
                dve.scalar_tensor_tensor(out=part, in0=banks[(OPA_BANK, OPB_BANK)[half][i]][:, :],
                                         scalar=rstd[:, 2 + 2 * half + c:3 + 2 * half + c], in1=part,
                                         op0=ALU.mult, op1=ALU.add).then_inc(x1_ready, 1)

            for i in range(len(PAIRS)):
                if i == A_PAIRS:
                    outputs_of(i - 1)
                    scaled_rows(4, (1, 2), 2 * KC, (0, 2))
                row_max(i, 0)
                row_max(i, 1)
                if i >= 1 and i != A_PAIRS:
                    outputs_of(i - 1)
                dve.wait_ge(prob_turned, 2 * i + 1)
                if i >= 1:
                    dve.wait_ge(pv_done, i)
                dve.tensor_copy(probT[:, 0, :, :].rearrange("p c k -> p (c k)"), banks[PT_BANK[0]][:, :])\
                   .then_inc(probTa_ready, 1)
                if i < A_PAIRS:
                    rotate_b(6 + i)
                else:
                    onto_stream(0, i - A_PAIRS)
            outputs_of(len(PAIRS) - 1)
            scaled_rows(6, (3, 4), 2 * KC, (4, 6))
            for i in range(4):
                onto_stream(1, i)
            scaled_rows(8, (1, 2, 3, 4), KC)

            n_step = 0

            def step(ins):
                nonlocal n_step
                n_step += 1
                ins.then_inc(r_step, 1)
                dve.wait_ge(r_step, n_step)

            dve.wait_ge(rstd_done, 4)
            for b in range(2):
                dve.memset(scan[:, b, :, 0:E // 2], 0.0)
            dve.wait_ge(logits_done, 1)
            dve.wait_ge(brt_in, 16)
            for c in range(TC):
                last = dve.scalar_tensor_tensor(out=lg[:, c, :], in0=banks[5][:, c * E:(c + 1) * E],
                                                scalar=rstd[:, 6 + c:7 + c], in1=brt[:, :], op0=ALU.mult, op1=ALU.add)
            step(last)
            for c in range(TC):
                last = dve.max(m8[:, c, :], lg[:, c, :])
            step(last)
            step(dve.tensor_scalar(nv0[:, :], m8[:, :, 0], -1.0, None, ALU.mult))
            assert n_step == R_MAX
            kth = m8[:, :, TOP_K - 1:TOP_K].broadcast_to([P, TC, E])
            pad = E // 2
            dve.tensor_tensor(gt[:, :, :], lg[:, :, :], kth, ALU.is_gt)
            dve.tensor_tensor(eq[:, :, :], lg[:, :, :], kth, ALU.is_equal)
            step(dve.tensor_tensor(scan[:, 0, :, pad:], lg[:, :, :], kth, ALU.is_equal))
            step(dve.tensor_reduce(more[:, :], gt[:, :, :], AX.X, ALU.add))
            step(dve.tensor_scalar(room[:, :], more[:, :], -1.0, float(TOP_K), ALU.mult, ALU.add))
            b = 0
            for shift in (1, 2, 4, 8, 16):
                step(dve.tensor_tensor(scan[:, 1 - b, :, pad:], scan[:, b, :, pad:],
                                       scan[:, b, :, pad - shift:pad + E - shift], ALU.add))
                b = 1 - b
            step(dve.tensor_tensor(ew[:, :, :], scan[:, b, :, pad:], room[:, :].unsqueeze(2).broadcast_to([P, TC, E]),
                                   ALU.is_le))
            step(dve.tensor_tensor(ew[:, :, :], ew[:, :, :], eq[:, :, :], ALU.mult))
            step(dve.tensor_tensor(sel[:, :, :], ew[:, :, :], gt[:, :, :], ALU.add))
            assert n_step == R_SEL
            dve.wait_ge(exp_ready, 1)
            step(dve.tensor_tensor(ew[:, :, :], ex[:, :, :], sel[:, :, :], ALU.mult))
            step(dve.tensor_reduce(den[:, :], ew[:, :, :], AX.X, ALU.add))
            step(dve.reciprocal(rden[:, :], den[:, :]))
            step(dve.tensor_tensor(wt[:, :, :], ew[:, :, :], rden[:, :].unsqueeze(2).broadcast_to([P, TC, E]), ALU.mult))
            dve.wait_ge(ranks_done, 1)
            count = banks[6][0:E, 2 * E:2 * E + 1]
            dve.tensor_scalar(npass[:, 0:1], count, float(SLOTS), 1.0, ALU.is_gt, ALU.add)
            dve.tensor_scalar(npass[:, 1:2], count, float(2 * SLOTS), None, ALU.is_gt)
            step(dve.tensor_scalar(npass[:, 2:3], count, float(3 * SLOTS), None, ALU.is_gt))
            step(dve.tensor_reduce(npass[:, 3:4], npass[:, 0:3], AX.X, ALU.add))
            assert n_step == R_NPASS
            step(dve.scalar_tensor_tensor(out=rk[:, :, :], in0=banks[6][:, 0:TC * E].rearrange("p (c e) -> p c e", c=TC),
                                          scalar=-NOT_ROUTED, in1=sel[:, :, :], op0=ALU.add, op1=ALU.mult))
            step(dve.tensor_scalar(rkc[:, :, :], rk[:, :, :], NOT_ROUTED, None, ALU.add))
            assert n_step == R_WT
            dve.wait_ge(cum_done, 1)
            step(dve.tensor_copy(cum[:, 0:1], banks[0][0:E, 0:1]))
            step(dve.tensor_tensor(cum[:, 1:2], cum[:, 0:1], npass[:, 3:4], ALU.subtract))
            numbers = iota[0:E, 0:TABLE]
            step(dve.tensor_scalar(ohA[:, :], numbers, cum[:, 0:1], None, ALU.is_ge))
            step(dve.scalar_tensor_tensor(out=oh[:, :], in0=numbers, scalar=cum[:, 1:2], in1=ohA[:, :],
                                          op0=ALU.is_ge, op1=ALU.subtract))
            step(dve.tensor_scalar(ohz[:, :], oh[:, :], cum[:, 1:2], None, ALU.mult))
            dve.wait_ge(turned_done, 1)
            step(dve.tensor_copy(rT[:, :, :].rearrange("e j s -> e (j s)"), banks[1][0:E, :]))
            assert n_step == R_PICK
            dve.wait_ge(picks_done, 1)
            dve.tensor_copy(tab[:, :], banks[2][0:1, 0:1 + E]).then_inc(tab_ready, 1)
            dve.wait_ge(p64_ready, 1)
            step(dve.scalar_tensor_tensor(out=base[:, :], in0=banks[2][:, 128:128 + TABLE], scalar=float(SLOTS),
                                          in1=p64[:, :], op0=ALU.mult, op1=ALU.subtract))
            pick = banks[2][:, 192:192 + 4 * TABLE].rearrange("p (j c q) -> p j c q", j=2, c=TC)
            step(dve.tensor_tensor(slot_p[:, :, :], pick[:, 0], base[:, :].unsqueeze(1).broadcast_to([P, TC, TABLE]),
                                   ALU.add))
            step(dve.tensor_copy(gate_p[:, :, :], pick[:, 1]))
            assert n_step == R_PSUM

            def slots_of(p):
                for c in range(TC):
                    last = dve.tensor_scalar(S[:, c, :], iota, slot_p[:, c, bass.ds(p, 1)], None, ALU.is_equal)
                last.then_inc(S_ready, 1)

            def gated_slots_of(p):
                for c in range(TC):
                    last = dve.tensor_scalar(G[:, c, :], iota_twice, slot_p[:, c, bass.ds(p, 1)],
                                             gate_p[:, c, bass.ds(p, 1)], ALU.is_equal, ALU.mult)
                last.then_inc(G_ready, 1)

            ffn_gain = gains[:, KC:2 * KC].rearrange("p (h m) -> p m h", h=2).unsqueeze(3)\
                .broadcast_to([P, KC // 2, 2, SLOTS])

            def tokens_out(n):
                dve.wait_ge(xrow_turned, n)
                dve.tensor_tensor(xT.rearrange("p (m h s) -> p m h s", h=2, s=SLOTS),
                                  banks[0][:, :].rearrange("p (m h s) -> p m h s", h=2, s=SLOTS), ffn_gain, ALU.mult)\
                   .then_inc(xT_ready, 1)

            def with_bias(dst, bank, j, p):
                for half in range(2):
                    b = bias_p[:, j, half * 4:half * 4 + 4, bass.ds(p, 1)].broadcast_to([P, FC // 2, SLOTS])

                    def part(t):
                        return t.rearrange("p (m h s) -> p h m s", m=FC // 2, h=2)[:, half]
                    last = dve.tensor_tensor(part(dst), part(banks[bank][:, :]), b, ALU.add)
                return last

            def add_up(p, tiles):
                for i in tiles:
                    c, n = i // 2, i % 2
                    part = acc[:, c, n * 512:(n + 1) * 512]
                    dve.wait_ge(spread[i], p)
                    dve.wait_ge(added[i], p)
                    dve.tensor_tensor(part, banks[SP_BANK[i]][:, :], part, ALU.add).then_inc(added[i], 1)

            slots_of(0)
            tokens_out(1)

            def one_pass(p, first):
                if first:
                    dve.wait_ge(biases_done, 1)
                    dve.tensor_copy(bias_p[:, 0, :, :].rearrange("p m q -> p (m q)"), banks[3][:, 0:FC * TABLE])\
                       .then_inc(biasg_ready, 1)
                    dve.wait_ge(biasg_ready, 1)
                dve.wait_ge(gate_turned, p + 1)
                with_bias(g, 4, 0, p).then_inc(gate_biased, 1)
                dve.wait_ge(gate_biased, p + 1)
                dve.tensor_scalar(g, g, LIMIT, None, ALU.min).then_inc(gate_clamped, 1)
                dve.wait_ge(gathered, p + 1)
                slots_of(p + 1)
                if not first:
                    dve.wait_ge(G_turned, p)
                gated_slots_of(p)
                dve.wait_ge(gate_clamped, p + 1)
                dve.wait_ge(sig_ready, p + 1)
                dve.tensor_tensor(sg, g, sg, ALU.mult).then_inc(gs_ready, 1)
                if not first:
                    add_up(p, (1, 2, 3))
                if first:
                    dve.wait_ge(biasu_ready, 1)
                dve.wait_ge(up_turned, p + 1)
                with_bias(u_t, 5, 1, p).then_inc(up_biased, 1)
                dve.wait_ge(up_biased, p + 1)
                dve.tensor_scalar(u_t, u_t, -LIMIT, LIMIT, ALU.max, ALU.min).then_inc(up_clamped, 1)
                dve.wait_ge(up_clamped, p + 1)
                dve.wait_ge(gs_ready, p + 1)
                if not first:
                    dve.wait_ge(unit_used[UNITS - 1], p)
                dve.scalar_tensor_tensor(out=act_t, in0=u_t, scalar=1.0, in1=sg, op0=ALU.add, op1=ALU.mult)\
                   .then_inc(act_ready, 1)
                if not first:
                    add_up(p, (0,))
                tokens_out(p + 2)

            dve.wait_ge(tab_ready, 1)
            passes = dve.value_load(tab[0:1, E:1 + E], min_val=1, max_val=MAX_PASSES)
            one_pass(0, True)
            halfway = dve.value_load(tab[0:1, HALFWAY:HALFWAY + 1], min_val=HALFWAY, max_val=MAX_PASSES)
            with dve.Fori(1, halfway) as p:
                one_pass(p, False)
            for i in range(4):
                c, n = i // 2, i % 2
                part = acc[:, c, n * 512:(n + 1) * 512]
                dve.wait_ge(bdown_done, i + 1)
                dve.wait_ge(added[i], halfway)
                dve.tensor_tensor(part, banks[SP_BANK[i]][:, :], part, ALU.add).then_inc(bias_added, 1)
            dve.wait_ge(bias_added, 4)
            with dve.Fori(halfway, passes) as p:
                one_pass(p, False)
            add_up(passes, range(4))

            dve.wait_ge(fgain_in, 16)
            for c in range(TC):
                dve.wait_ge(rstd_done, 5 + c)
                dve.scalar_tensor_tensor(out=xs[:, c, :], in0=acc[:, c, :], scalar=rstd[:, 8 + c:9 + c],
                                         in1=fgain, op0=ALU.mult, op1=ALU.mult).then_inc(fin_ready, 1)


INS = ("x", "attn_norm", "w_in", "q_norm", "k_norm", "out_norm_a", "out_norm_b", "w_out", "ffn_norm",
       "w_router", "b_router", "w_gate", "b_gate", "w_up", "b_up", "w_down", "b_down", "final_norm")


def kernel(**inputs):
    import concourse.bacc as bacc
    from concourse.bass_utils import run_bass_kernel_spmd

    nc = bacc.Bacc("TRN2", target_bir_lowering=False, num_devices=1)
    arrays, args = {}, []
    for name in INS:
        arrays[name] = np.ascontiguousarray(inputs[name])
    arrays["consts"] = constants()
    for name, a in arrays.items():
        args.append(nc.dram_tensor(name, a.shape, F32, kind="ExternalInput").ap())
    out = nc.dram_tensor("out", arrays["x"].shape, F32, kind="ExternalOutput").ap()
    encoder_kernel(nc, *args, out)
    r = run_bass_kernel_spmd(nc, [arrays], core_ids=[0])
    return r.results[0]["out"]
```
